# Optimizing a Trainium2 kernel written in Bass

```python
import jax, jax.numpy as jnp
from jax import lax
import numpy as np

D_MODEL = 1024
BATCH = 1
SEQ = 512
DEPTH = 1

CHUNK = 64
Q_BLOCK = 128
SB_HEADS = 8
SB_HEAD_DIM = 64
SB_WIDTH = SB_HEADS * SB_HEAD_DIM
RET_HEADS = 4
RET_KEY_DIM = 128
RET_VALUE_DIM = 128
RET_QK_WIDTH = RET_HEADS * RET_KEY_DIM
RET_V_WIDTH = RET_HEADS * RET_VALUE_DIM
D_FF = 4 * D_MODEL
RMS_EPS = 1e-6
GN_EPS = 1e-5
ROPE_BASE = 10000.0

SPLIT_SIZES = (SB_WIDTH, SB_WIDTH, SB_WIDTH,
               RET_QK_WIDTH, RET_QK_WIDTH, RET_V_WIDTH, RET_V_WIDTH,
               D_MODEL, D_MODEL)
SPLIT_POINTS = tuple(int(p) for p in np.cumsum(SPLIT_SIZES)[:-1])
W_IN_COLS = int(sum(SPLIT_SIZES))

kernel_name = "sandwich_macaron_stickbreak_retention_hybrid"

def rms_norm(x, g):
    xf = x.astype(jnp.float32)
    y = xf * lax.rsqrt(jnp.mean(xf * xf, axis=-1, keepdims=True) + RMS_EPS)
    return (y * g.astype(jnp.float32)).astype(x.dtype)

def swiglu(h, w_gate, w_up, w_down):
    return (jax.nn.silu(h @ w_gate) * (h @ w_up)) @ w_down

def rotary(x, pos):
    half = x.shape[-1] // 2
    inv_freq = ROPE_BASE ** (-jnp.arange(half, dtype=jnp.float32) / half)
    ang = pos[:, None] * inv_freq[None, :]
    cos = jnp.cos(ang)[None, :, None, :]
    sin = jnp.sin(ang)[None, :, None, :]
    x1, x2 = x[..., :half], x[..., half:]
    return jnp.concatenate([x1 * cos - x2 * sin, x1 * sin + x2 * cos], axis=-1)

def stick_breaking_attention(q, k, v):
    seq = q.shape[1]
    scale = q.shape[-1] ** -0.5
    outs = []
    for i in range(seq // Q_BLOCK):
        start, end = i * Q_BLOCK, (i + 1) * Q_BLOCK
        qb = q[:, start:end]
        kb = k[:, :end]
        vb = v[:, :end]
        z = jnp.einsum('bqhd,bkhd->bhqk', qb, kb) * scale
        t_pos = start + jnp.arange(Q_BLOCK)
        s_pos = jnp.arange(end)
        causal = s_pos[None, :] < t_pos[:, None]
        log_keep = jnp.where(causal, jax.nn.log_sigmoid(-z), 0.0)
        suffix = lax.cumsum(log_keep, axis=3, reverse=True)
        between = jnp.concatenate(
            [suffix[..., 1:], jnp.zeros_like(suffix[..., :1])], axis=-1)
        w = jnp.where(causal, jnp.exp(jax.nn.log_sigmoid(z) + between), 0.0)
        outs.append(jnp.einsum('bhqk,bkhd->bqhd', w, vb))
    return jnp.concatenate(outs, axis=1)

def retention_chunkwise(q, k, v, log_gamma):
    b, seq, h, dk = q.shape
    dv = v.shape[-1]
    n = seq // CHUNK
    qc = q.reshape(b, n, CHUNK, h, dk)
    kc = k.reshape(b, n, CHUNK, h, dk)
    vc = v.reshape(b, n, CHUNK, h, dv)
    idx = jnp.arange(CHUNK, dtype=jnp.float32)
    diff = idx[:, None] - idx[None, :]
    inner_decay = jnp.where(diff[None] >= 0,
                            jnp.exp(jnp.maximum(diff, 0.0)[None] * log_gamma[:, None, None]),
                            0.0)
    scores = jnp.einsum('bnchd,bnmhd->bnhcm', qc, kc) * inner_decay
    inner = jnp.einsum('bnhcm,bnmhe->bnche', scores, vc)
    k_decay = jnp.exp((CHUNK - 1 - idx)[:, None] * log_gamma[None, :])
    chunk_kv = jnp.einsum('bnmhd,bnmhe->nbhde', kc * k_decay[None, None, :, :, None], vc)
    chunk_decay = jnp.exp(CHUNK * log_gamma)[None, :, None, None]

    def step(state, kv):
        return chunk_decay * state + kv, state

    _, prev_states = lax.scan(step, jnp.zeros((b, h, dk, dv), jnp.float32), chunk_kv)
    q_decay = jnp.exp((idx + 1.0)[:, None] * log_gamma[None, :])
    cross = jnp.einsum('bnchd,nbhde->bnche', qc * q_decay[None, None, :, :, None], prev_states)
    return (inner + cross).reshape(b, seq, h, dv)

def head_group_norm(o):
    mu = jnp.mean(o, axis=-1, keepdims=True)
    var = jnp.mean(jnp.square(o - mu), axis=-1, keepdims=True)
    return (o - mu) * lax.rsqrt(var + GN_EPS)

def setup_inputs(seed: int = 0) -> dict:
    key = jax.random.key(seed)
    ks = jax.random.split(key, 20)

    def dense(k, fan_in, fan_out):
        return jax.random.normal(k, (DEPTH, fan_in, fan_out), jnp.float32) * fan_in ** -0.5

    def gain(k):
        return 1.0 + 0.02 * jax.random.normal(k, (DEPTH, D_MODEL), jnp.float32)

    return {
        "x": jax.random.normal(ks[0], (BATCH, SEQ, D_MODEL), jnp.float32),
        "g_ffn1_pre": gain(ks[1]),
        "g_ffn1_post": gain(ks[2]),
        "w_ffn1_gate": dense(ks[3], D_MODEL, D_FF),
        "w_ffn1_up": dense(ks[4], D_MODEL, D_FF),
        "w_ffn1_down": dense(ks[5], D_FF, D_MODEL),
        "g_mix_pre": gain(ks[6]),
        "w_in": dense(ks[7], D_MODEL, W_IN_COLS),
        "w_proj_sb": dense(ks[8], SB_WIDTH, D_MODEL),
        "w_proj_ret": dense(ks[9], RET_V_WIDTH, D_MODEL),
        "w_out": dense(ks[10], D_MODEL, D_MODEL),
        "g_mix_post": gain(ks[11]),
        "g_ffn2_pre": gain(ks[12]),
        "g_ffn2_post": gain(ks[13]),
        "w_ffn2_gate": dense(ks[14], D_MODEL, D_FF),
        "w_ffn2_up": dense(ks[15], D_MODEL, D_FF),
        "w_ffn2_down": dense(ks[16], D_FF, D_MODEL),
    }

def reference(x, g_ffn1_pre, g_ffn1_post, w_ffn1_gate, w_ffn1_up, w_ffn1_down,
              g_mix_pre, w_in, w_proj_sb, w_proj_ret, w_out, g_mix_post,
              g_ffn2_pre, g_ffn2_post, w_ffn2_gate, w_ffn2_up, w_ffn2_down):
    b, seq, _ = x.shape
    f32 = jnp.float32
    pos = jnp.arange(seq, dtype=f32)
    log_gamma = jnp.log(1.0 - 2.0 ** (-5.0 - jnp.arange(RET_HEADS, dtype=f32)))

    for l in range(DEPTH):
        h = rms_norm(x, g_ffn1_pre[l])
        x = x + 0.5 * rms_norm(swiglu(h, w_ffn1_gate[l], w_ffn1_up[l], w_ffn1_down[l]),
                               g_ffn1_post[l])

        h = rms_norm(x, g_mix_pre[l])
        proj = h @ w_in[l]
        (q_sb, k_sb, v_sb, q_r, k_r, v_r, g_r,
         gate_sb, gate_ret) = jnp.split(proj, SPLIT_POINTS, axis=-1)

        shp_sb = (b, seq, SB_HEADS, SB_HEAD_DIM)
        o_sb = stick_breaking_attention(q_sb.reshape(shp_sb).astype(f32),
                                        k_sb.reshape(shp_sb).astype(f32),
                                        v_sb.reshape(shp_sb).astype(f32))
        o_sb = o_sb.reshape(b, seq, SB_WIDTH).astype(x.dtype)

        shp_qk = (b, seq, RET_HEADS, RET_KEY_DIM)
        qr = rotary(q_r.reshape(shp_qk).astype(f32), pos)
        kr = rotary(k_r.reshape(shp_qk).astype(f32), pos) * RET_KEY_DIM ** -0.5
        vr = v_r.reshape(b, seq, RET_HEADS, RET_VALUE_DIM).astype(f32)
        o_r = head_group_norm(retention_chunkwise(qr, kr, vr, log_gamma))
        o_r = (o_r.reshape(b, seq, RET_V_WIDTH) * jax.nn.silu(g_r.astype(f32))).astype(x.dtype)

        merged = (jax.nn.sigmoid(gate_sb) * (o_sb @ w_proj_sb[l])
                  + jax.nn.sigmoid(gate_ret) * (o_r @ w_proj_ret[l]))
        x = x + rms_norm(merged @ w_out[l], g_mix_post[l])

        h = rms_norm(x, g_ffn2_pre[l])
        x = x + 0.5 * rms_norm(swiglu(h, w_ffn2_gate[l], w_ffn2_up[l], w_ffn2_down[l]),
                               g_ffn2_post[l])
    return x


_drawn_inputs = setup_inputs


def setup_inputs(seed=0):
    import zlib

    import numpy as np

    out = dict(_drawn_inputs(seed))
    spreads = {}
    factors = {'g_ffn1_pre': 2.904,
     'g_ffn1_post': 4.391,
     'g_mix_post': 11.022,
     'g_ffn2_pre': 19.849,
     'g_ffn2_post': 33.831}
    for name, (base, spread) in spreads.items():
        noise = np.random.default_rng([zlib.crc32(name.encode()), seed]).standard_normal(out[name].shape)
        drawn = base * np.exp(spread * noise) if base else spread * noise
        out[name] = __import__('jax').numpy.asarray(drawn.astype(out[name].dtype))
    for name, factor in factors.items():
        out[name] = (out[name] * factor).astype(out[name].dtype)
    return out
```

```python
from contextlib import ExitStack

import numpy as np

import concourse.bass as bass
from concourse import mybir

ALU = mybir.AluOpType
ACT = mybir.ActivationFunctionType
F32 = mybir.dt.float32
F32R = mybir.dt.float32r

P = 128
T = 512
D = 1024
KD = D // P
TT = T // P
FF = 4096
NF = FF // P
SBH, SBD = 8, 64
RH, RD = 4, 128
PAIRS = SBH * SBD // P
RMS_EPS, GN_EPS = 1e-6, 1e-5
ARENA = 212832
UNIT = KD * P
SLOTS = 4
AHEAD = 2

U_UP1 = 0
U_DOWN1 = U_UP1 + 2 * NF
U_V = U_DOWN1 + NF
U_HEADS = U_V + 8
U_MERGE = U_HEADS + 5 * PAIRS
U_OUT = U_MERGE + 4 * KD
U_UP2 = U_OUT + KD
U_DOWN2 = U_UP2 + 2 * NF
U_END = U_DOWN2 + NF

C_QSB, C_KSB, C_VSB, C_QR, C_KR, C_VR, C_GR, C_GATE_SB, C_GATE_RET = 0, 4, 8, 12, 16, 20, 24, 28, 36

IDENT, ONES, MEAN, NEG_TRI, NEG_ONES, EPS = 0, 128, 256, 384, 512, 640
CONST_COLS = 642


def constants():
    p = np.arange(P)
    c = np.zeros((P, CONST_COLS), np.float32)
    c[:, IDENT:IDENT + P] = np.eye(P)
    c[:, ONES:ONES + P] = 1.0
    c[:, MEAN:MEAN + P] = 1.0 / RD
    c[:, NEG_TRI:NEG_TRI + P] = np.where(p[:, None] >= p[None, :], -1.0, 0.0)
    c[:, NEG_ONES:NEG_ONES + P] = -1.0
    c[:, EPS] = RMS_EPS
    c[:, EPS + 1] = GN_EPS
    log_gamma = np.log(1.0 - 2.0 ** (-5.0 - np.arange(RH)))
    lag = np.arange(T)[None, :] - p[:, None]
    decay = np.where(lag[:, None] >= 0, np.exp(np.maximum(lag, 0)[:, None] * log_gamma[None, :, None]), 0.0)
    decay = (decay * RD ** -0.5).astype(np.float32)
    half = RD // 2
    inv = (np.float32(10000.0) ** (-np.arange(half, dtype=np.float32) / np.float32(half))).astype(np.float32)
    ang = (np.arange(T, dtype=np.float32)[None, :] * inv[:, None]).astype(np.float32)
    cos, sin = np.cos(ang.astype(np.float64)), np.sin(ang.astype(np.float64))
    rope = np.stack([np.concatenate([cos, cos]), np.concatenate([sin, -sin])], 1).astype(np.float32)
    return c, decay, rope


def schedule_heads():
    events = []
    for step in range(PAIRS + 1):
        fill = [("mm", 5 * step + j, k) for j in range(5) for k in range(KD)] if step < PAIRS else []
        att = []
        if step >= 1:
            p = step - 1
            tiles = [(p, hh, b) for hh in range(3) for b in reversed(range(TT))]
            for n in range(len(tiles) + 3):
                group = []
                if n < len(tiles):
                    group.append(("z", tiles[n]))
                if 2 <= n < len(tiles) + 2 and tiles[n - 2][1] < 2:
                    group.append(("s", tiles[n - 2]))
                if n >= 3:
                    group.append(("o", tiles[n - 3]))
                if n == 11:
                    group.append(("sb_out", p))
                if p >= 1 and n in (1, 3, 5, 7):
                    group.append(("gn" + "_ABCD"[(n + 1) // 2], p - 1))
                att.append(group)
            if step == PAIRS:
                att += [[("gn" + x, p)] for x in "ABCD"]
        share = -(-len(fill) // len(att)) if att else len(fill)
        for i in range(max(len(att), 1)):
            events += att[i] if att else []
            events += fill[i * share:(i + 1) * share]
    return events


def build(nc, x, gains, w_gate1, w_up1, w_down1, w_in, w_proj_sb, w_proj_ret, w_out,
          w_gate2, w_up2, w_down2, const, decay_t, rope_t, out):
    with ExitStack() as ctx:
        base = -(-nc.sbuf_base // 32) * 32
        ctx.enter_context(nc.sbuf_tensor("arena", [P, ARENA // 4], F32))
        top = [0]

        def place(name, shape, dt=F32, at=None):
            size = -(-int(np.prod(shape[1:])) * 4 // 32) * 32
            off = top[0] if at is None else at
            if at is None:
                top[0] += size
            assert off + size <= ARENA, (name, off + size)
            return nc.alloc_sbuf_tensor_at(name, shape, dt, offset=base + off), off + size

        xs, _ = place("xs", [P, KD, T])
        h_hi, _ = place("h_hi", [P, KD, T], F32R)
        h_lo, _ = place("h_lo", [P, KD, T], F32R)
        w_raw, _ = place("w_raw", [P, SLOTS, UNIT])
        w_hi, _ = place("w_hi", [P, SLOTS, UNIT], F32R)
        w_lo, _ = place("w_lo", [P, SLOTS, UNIT], F32R)
        cst, _ = place("cst", [P, CONST_COLS])
        gcol, _ = place("gcol", [P, 6, KD])
        std, _ = place("std", [P, TT])
        rstd, _ = place("rstd", [P, TT])
        decay, _ = place("decay", [P, RH, T])
        rope, _ = place("rope", [P, 2, T])
        region = top[0]
        act, e = place("act", [P, NF, T], at=region)
        a_hi, e = place("a_hi", [P, 2, T], F32R, at=e)
        a_lo, e = place("a_lo", [P, 2, T], F32R, at=e)
        gate_s, e = place("gate_s", [P, 2, T], at=e)
        ys, e2 = place("ys", [P, KD, T], at=region)
        sq, e2 = place("sq", [P, 2, T], at=e2)
        hf, e2 = place("hf", [P, 2, T], at=e2)
        diag, e2 = place("diag", [P, TT, P], at=e2)
        x_tok, _ = place("x_tok", [P, TT, D], at=e2)
        g_tok, _ = place("g_tok", [6 * KD, P], at=e)
        v_sb, e3 = place("v_sb", [P, TT, T], at=region)
        v_r, e3 = place("v_r", [P, TT, T], at=e3)
        qk_hi, e3 = place("qk_hi", [P, 2, 2, T], F32R, at=e3)
        qk_lo, e3 = place("qk_lo", [P, 2, 2, T], F32R, at=e3)
        qk_r, e3 = place("qk_r", [P, 2, 2, T], at=e3)
        g_r, e3 = place("g_r", [P, 2, T], at=e3)
        lt, e3 = place("lt", [P, 2, T], at=e3)
        sp, e3 = place("sp", [P, 2, T], at=e3)
        cum, e3 = place("cum", [P, 2, T - P], at=e3)
        wt, e3 = place("wt", [P, 2, T], at=e3)
        ropeB, e3 = place("ropeB", [P, T], at=e3)
        gn_c, e3 = place("gn_c", [P, T], at=e3)
        gn_t, e3 = place("gn_t", [P, T], at=e3)
        oe = ARENA - 4 * PAIRS * T * 4
        assert e3 <= oe
        o_sb_hi, e4 = place("o_sb_hi", [P, PAIRS, T], F32R, at=oe)
        o_sb_lo, e4 = place("o_sb_lo", [P, PAIRS, T], F32R, at=e4)
        o_r_hi, e4 = place("o_r_hi", [P, RH, T], F32R, at=e4)
        o_r_lo, e4 = place("o_r_lo", [P, RH, T], F32R, at=e4)
        me = e2
        m_hi, e5 = place("m_hi", [P, KD, T], F32R, at=me)
        m_lo, e5 = place("m_lo", [P, KD, T], F32R, at=e5)
        assert e5 <= oe, (e5, oe)
        sig, e6 = place("sig", [P, 4, T], at=region)
        tm, e6 = place("tm", [P, 2, 2, T], at=e6)
        assert e6 <= me

        ps = ctx.enter_context(nc.psum_tensor("ps", [P, 8, T], F32))

        def sem(name):
            return ctx.enter_context(nc.semaphore(name))

        raw_full = [sem(f"raw_full{i}") for i in range(SLOTS)]
        w_hi_done, w_lo_done, unit_done = sem("w_hi_done"), sem("w_lo_done"), sem("unit_done")
        const_in, gains_in, tables_in = sem("const_in"), sem("gains_in"), sem("tables_in")
        x_in = [sem(f"x_in{t}") for t in range(TT)]
        gains_t, gains_ok = sem("gains_t"), sem("gains_ok")
        xt_done, x_copied = sem("xt_done"), sem("x_copied")
        silu_done, a_done, a_hi_done, a_lo_done = sem("silu_done"), sem("a_done"), sem("a_hi_done"), sem("a_lo_done")
        y_ready, y_copied, y_scaled = sem("y_ready"), sem("y_copied"), sem("y_scaled")
        sq_ready, sq_used, std_ready, rstd_ready = sem("sq_ready"), sem("sq_used"), sem("std_ready"), sem("rstd_ready")
        diag_ready, r_ready, x_ready = sem("diag_ready"), sem("r_ready"), sem("x_ready")
        hf_ready, h_hi_done, h_lo_done = sem("hf_ready"), sem("h_hi_done"), sem("h_lo_done")
        v_ready, v_copied = sem("v_ready"), sem("v_copied")
        q_hi_done, q_lo_done, rope_mul, rope_done, g_copied = (
            sem("q_hi_done"), sem("q_lo_done"), sem("rope_mul"), sem("rope_done"), sem("g_copied"))
        z_ready, l_step, sp_raw, sp_ready, cum_done, s_done = (
            sem("z_ready"), sem("l_step"), sem("sp_raw"), sem("sp_ready"), sem("cum_done"), sem("s_done"))
        w_raw_done, w_masked, w_ret, o_done = sem("w_raw_done"), sem("w_masked"), sem("w_ret"), sem("o_done")
        osb_hi_done, osb_lo_done = sem("osb_hi_done"), sem("osb_lo_done")
        gn_copied, gn_mean, gn_centred, gn_squared, gn_var, gn_std, gn_silu = (
            sem("gn_copied"), sem("gn_mean"), sem("gn_centred"), sem("gn_squared"), sem("gn_var"), sem("gn_std"),
            sem("gn_silu"))
        gn_v, or_hi_done, or_lo_done = sem("gn_v"), sem("or_hi_done"), sem("or_lo_done")
        sig_done, tm_done, m_done, m_hi_done, m_lo_done = (
            sem("sig_done"), sem("tm_done"), sem("m_done"), sem("m_hi_done"), sem("m_lo_done"))
        out_t, out_stored = sem("out_t"), sem("out_stored")
        out_copied = [sem("out_copied_v"), sem("out_copied_s")]

        def wait(eng, s, value):
            if isinstance(value, int) and value <= 0:
                return
            eng.wait_ge(s, value)

        def c(col, n=P):
            return cst[:, col:col + n]

        events = schedule_heads()
        score_tiles = [e[1] for e in events if e[0] == "z"]
        sb_tiles = [t for t in score_tiles if t[1] < 2]
        ret_tiles = [t for t in score_tiles if t[1] == 2]
        o_tiles = [e[1] for e in events if e[0] == "o"]
        s_tiles = [e[1] for e in events if e[0] == "s"]
        assert o_tiles == score_tiles and s_tiles == sb_tiles

        OUT_BANK = (2, 3, 4, 5, 6, 7, 0, 1)
        O_SB, O_RET, FILL = 4, 5, 6

        def half_units(stage_unit):
            return UNIT // 2 if stage_unit % 4 >= 2 else UNIT

        def unit_cols(u):
            return half_units(u - U_MERGE) if U_MERGE <= u < U_OUT else UNIT

        block = ctx.enter_context(nc.Block())

        @block.sync
        def _(sp_eng):
            def load(u, slot, src, cols=UNIT):
                wait(sp_eng, w_lo_done, u - (SLOTS - 1))
                dst = w_raw[:, slot, 0:cols].rearrange("p (k c) -> p k c", k=src.shape[1])
                sp_eng.dma_start(dst, src).then_inc(raw_full[slot], 16)

            def cols(w, f):
                return w.rearrange("(k p) c -> p k c", p=P)[:, :, bass.ts(f, P)]

            def ffn_loads(u0, wg, wu, wd):
                def up(i):
                    for j in range(2):
                        load(i * 2 + u0 + 2 * j, 2 * j, cols(wg, i + j))
                        load(i * 2 + u0 + 2 * j + 1, 2 * j + 1, cols(wu, i + j))

                def down(i):
                    for j in range(SLOTS):
                        load(i + u0 + 2 * NF + j, j, wd[bass.ts(i + j, P), :].rearrange("p (k c) -> p k c", k=KD))

                up(0)
                with sp_eng.Fori(1, NF // 2) as turn:
                    i = turn * 2
                    up(i)
                with sp_eng.Fori(0, NF // SLOTS) as turn:
                    i = turn * SLOTS
                    down(i)

            ffn_loads(U_UP1, w_gate1, w_up1, w_down1)
            u = U_V
            for c0 in (C_VSB, C_VR):
                for j in range(4):
                    src = w_in[2 * j * P:(2 * j + 2) * P, c0 * P:c0 * P + T].rearrange("(k p) c -> p k c", p=P)
                    load(u, u % SLOTS, src)
                    u += 1
            for s in range(PAIRS):
                for c0 in (C_QSB, C_KSB, C_QR, C_KR, C_GR):
                    load(u, u % SLOTS, cols(w_in, c0 + s))
                    u += 1
            with sp_eng.Fori(0, KD) as d:
                load(d * 4 + U_MERGE, 0, cols(w_in, d + C_GATE_SB))
                load(d * 4 + U_MERGE + 1, 1, cols(w_in, d + C_GATE_RET))
                load(d * 4 + U_MERGE + 2, 2, cols(w_proj_sb, d), UNIT // 2)
                load(d * 4 + U_MERGE + 3, 3, cols(w_proj_ret, d), UNIT // 2)
            for d in range(KD):
                load(U_OUT + d, d % SLOTS, cols(w_out, d))
            ffn_loads(U_UP2, w_gate2, w_up2, w_down2)
            for n in range(2 * TT):
                half, t = n // TT, n % TT
                sp_eng.wait_ge(out_copied[n % 2], n // 2 + 1)
                sp_eng.dma_start(out[t * P:(t + 1) * P, half * T:(half + 1) * T],
                                 x_tok[:, t, half * T:(half + 1) * T]).then_inc(out_stored, 16)
            sp_eng.wait_ge(out_stored, 16 * 2 * TT)

        @block.tensor
        def _(pe):
            def evacuated(f):
                s, j = f // 5, f % 5
                if j < 2:
                    pe.wait_ge(q_lo_done, 2 * s + j + 1)
                elif j < 4:
                    pe.wait_ge(rope_mul, 3 * (2 * s + j - 2) + 3)
                else:
                    pe.wait_ge(g_copied, s + 1)

            def bank_read(i):
                tile = score_tiles[i]
                if tile[1] < 2:
                    pe.wait_ge(w_raw_done, sb_tiles.index(tile) + 1)
                else:
                    pe.wait_ge(w_ret, ret_tiles.index(tile) + 1)

            def product(bank, w_at, src_hi, src_lo, first, last, m=slice(None)):
                (slot, col) = w_at
                wh, wl = w_hi[:, slot, col:col + P], w_lo[:, slot, col:col + P]
                pe.matmul(ps[:, bank, :], wh, src_hi, start=first, stop=False)
                pe.matmul(ps[:, bank, :], wh, src_lo, start=False, stop=False)
                return pe.matmul(ps[:, bank, :], wl, src_hi, start=False, stop=last)

            def unit(u, slot, bank, hi, lo, nk=KD, each_k=None):
                pe.wait_ge(w_lo_done, u + 1)
                for k in range(nk):
                    if each_k is not None:
                        pe.wait_ge(each_k[0], each_k[1] + k + 1)
                    last = product(bank, (slot, k * P), hi[:, k, :], lo[:, k, :], k == 0, k == nk - 1)
                last.then_inc(unit_done, 1)

            def stats(n, s_bank, r_bank):
                for k in range(KD):
                    pe.wait_ge(sq_ready, KD * n + k + 1)
                    for j in range(TT):
                        mm = pe.matmul(ps[:, s_bank, j:j + 1], sq[:, k % 2, j * P:(j + 1) * P], c(ONES, 1),
                                       start=(k == 0 and j == 0), stop=(k == KD - 1), skip_group_check=True)
                    mm.then_inc(sq_used, 1)
                pe.wait_ge(diag_ready, n + 1)
                pe.matmul(ps[:, r_bank, :], c(ONES), diag[:, :, :].rearrange("p j t -> p (j t)"),
                          start=True, stop=True).then_inc(r_ready, 1)

            def ffn(fi, u0):
                def up(i, j, first):
                    f = i + j
                    each_k = (h_lo_done, 2 * KD * fi) if first and j == 0 else None
                    wait(pe, silu_done, f + NF * fi - 1)
                    unit(f * 2 + u0, 2 * j, 2 * j, h_hi, h_lo, each_k=each_k)
                    wait(pe, a_done, f + NF * fi - 1)
                    unit(f * 2 + u0 + 1, 2 * j + 1, 2 * j + 1, h_hi, h_lo)

                for j in range(2):
                    up(0, j, True)
                with pe.Fori(1, NF // 2) as turn:
                    i = turn * 2
                    for j in range(2):
                        up(i, j, False)

                def down(f, slot, banks, first=False, last=False):
                    pe.wait_ge(w_lo_done, f + u0 + 2 * NF + 1)
                    pe.wait_ge(a_lo_done, f + NF * fi + 1)
                    for d in banks:
                        if first and d == 0:
                            pe.wait_ge(a_done, NF * (fi + 1))
                        par = slot % 2
                        mm = product(d, (slot, d * P), a_hi[:, par, :], a_lo[:, par, :], first, last)
                        if last and d < KD - 1:
                            mm.then_inc(y_ready, 1)
                    mm.then_inc(unit_done, 1)

                down(0, 0, (4, 5, 6, 7, 0, 1, 2, 3), first=True)
                with pe.Fori(0, (NF - 3) // SLOTS) as turn:
                    i = turn * SLOTS + 1
                    for j in range(SLOTS):
                        down(i + j, (j + 1) % SLOTS, range(KD))
                for f in range(NF - 3, NF):
                    down(f, f % SLOTS, range(KD), last=(f == NF - 1))

            pe.wait_ge(const_in, 16)
            pe.wait_ge(gains_in, 16 * 6)
            pe.transpose(ps[:, 0, 0:6 * KD], g_tok[:, :], cst[0:6 * KD, IDENT:IDENT + 6 * KD]).then_inc(gains_t, 1)
            pe.wait_ge(gains_ok, 1)
            for k in range(KD):
                for t in range(TT):
                    if k == 0:
                        pe.wait_ge(x_in[t], 16)
                    mm = pe.transpose(ps[:, k, t * P:(t + 1) * P], x_tok[:, t, k * P:(k + 1) * P], c(IDENT))
                mm.then_inc(xt_done, 1)
            stats(0, 0, 5)
            ffn(0, U_UP1)
            stats(1, 0, 1)
            stats(2, 4, 5)

            for kind in range(2):
                for j in range(4):
                    u = U_V + 4 * kind + j
                    pe.wait_ge(w_lo_done, u + 1)
                    for kk in range(2):
                        k = 2 * j + kk
                        if kind == 0:
                            pe.wait_ge(h_lo_done, KD + k + 1)
                        for t in range(TT):
                            tok = slice(t * P, (t + 1) * P)
                            wc = slice(kk * T, (kk + 1) * T)
                            bank = ps[:, 4 * kind + t, :]
                            pe.matmul(bank, h_hi[:, k, tok], w_hi[:, u % SLOTS, wc], start=(k == 0), stop=False)
                            pe.matmul(bank, h_hi[:, k, tok], w_lo[:, u % SLOTS, wc], start=False, stop=False)
                            mm = pe.matmul(bank, h_lo[:, k, tok], w_hi[:, u % SLOTS, wc], start=False,
                                           stop=(k == KD - 1))
                            if k == KD - 1 and t < TT - 1:
                                mm.then_inc(v_ready, 1)
                    mm.then_inc(unit_done, 1)

            nz = ns = no = 0
            for ev in events:
                if ev[0] == "mm":
                    f, k = ev[1], ev[2]
                    u = U_HEADS + f
                    if k == 0:
                        pe.wait_ge(w_lo_done, u + 1)
                        if f < 2:
                            pe.wait_ge(v_copied, 8)
                        else:
                            evacuated(f - 2)
                    mm = product(FILL + f % 2, (u % SLOTS, k * P), h_hi[:, k, :], h_lo[:, k, :],
                                 k == 0, k == KD - 1)
                    if k == KD - 1:
                        mm.then_inc(unit_done, 1)
                elif ev[0] == "z":
                    p, hh, b = ev[1]
                    W = T - b * P
                    if b == TT - 1 and hh == 0:
                        pe.wait_ge(q_lo_done, 2 * p + 2)
                    if b == TT - 1 and hh == 2:
                        pe.wait_ge(rope_done, 2 * p + 2)
                    if nz >= 4:
                        bank_read(nz - 4)
                    bank = ps[:, nz % 4, 0:W]
                    keys, queries = slice(b * P, (b + 1) * P), slice(b * P, T)
                    if hh < 2:
                        r = slice(hh * SBD, (hh + 1) * SBD)
                        q_h, q_l = qk_hi[r, p % 2, 0, queries], qk_lo[r, p % 2, 0, queries]
                        k_h, k_l = qk_hi[r, p % 2, 1, keys], qk_lo[r, p % 2, 1, keys]
                        pe.matmul(bank, k_h, q_h, start=True, stop=False)
                        pe.matmul(bank, k_h, q_l, start=False, stop=False)
                        mm = pe.matmul(bank, k_l, q_h, start=False, stop=True)
                    else:
                        mm = pe.matmul(bank, qk_r[:, p % 2, 1, keys], qk_r[:, p % 2, 0, queries], start=True, stop=True)
                    mm.then_inc(z_ready, 1)
                    nz += 1
                elif ev[0] == "s":
                    p, hh, b = ev[1]
                    W = T - b * P
                    zi = score_tiles.index(ev[1])
                    pe.wait_ge(sp_ready, ns + 1)
                    mm = pe.matmul(ps[:, zi % 4, 0:W], c(NEG_TRI), sp[:, ns % 2, 0:W], start=False, stop=True,
                                   skip_group_check=True)
                    if b < TT - 1:
                        pe.wait_ge(cum_done, 3 * (ns // 4) + (TT - 1 - b))
                        mm = pe.matmul(ps[:, zi % 4, P:W], c(NEG_ONES), cum[:, (b + 1) % 2, b * P:T - P],
                                       start=False, stop=True, skip_group_check=True)
                    mm.then_inc(s_done, 1)
                    ns += 1
                elif ev[0] == "o":
                    p, hh, b = ev[1]
                    W = T - b * P
                    if hh < 2:
                        pe.wait_ge(w_masked, sb_tiles.index(ev[1]) + 1)
                        if hh == 0 and b == TT - 1 and p:
                            pe.wait_ge(osb_lo_done, p)
                        o = ps[hh * SBD:(hh + 1) * SBD, O_SB, b * P:T]
                        vv = v_sb[:, b, p * P + hh * SBD:p * P + (hh + 1) * SBD]
                    else:
                        pe.wait_ge(w_ret, ret_tiles.index(ev[1]) + 1)
                        if b == TT - 1 and p:
                            pe.wait_ge(gn_std, p)
                        o = ps[:, O_RET, b * P:T]
                        vv = v_r[:, b, p * P:(p + 1) * P]
                    pe.matmul(o, vv, wt[:, no % 2, 0:W], start=(b == TT - 1), stop=True,
                              skip_group_check=True).then_inc(o_done, 1)
                    no += 1
                elif ev[0] == "gnA":
                    pe.wait_ge(gn_copied, ev[1] + 1)
                    pe.matmul(ps[:, O_RET, :], c(MEAN), gn_t[:, :], start=True, stop=True).then_inc(gn_mean, 1)
                elif ev[0] == "gnB":
                    pe.wait_ge(gn_squared, ev[1] + 1)
                    pe.matmul(ps[:, O_RET, :], c(MEAN), gn_t[:, :], start=True, stop=True).then_inc(gn_var, 1)

            pe.wait_ge(osb_lo_done, PAIRS)
            pe.wait_ge(or_lo_done, RH)

            def merge(d, par, waits):
                for j, (hi, lo, nk) in enumerate(((h_hi, h_lo, KD), (h_hi, h_lo, KD),
                                                  (o_sb_hi, o_sb_lo, PAIRS), (o_r_hi, o_r_lo, RH))):
                    if waits and j < 2:
                        pe.wait_ge(sig_done, d * 2 - 3 + j)
                    if waits and j >= 2:
                        pe.wait_ge(tm_done, d * 2 - 5 + j)
                    unit(d * 4 + U_MERGE + j, j, 4 * par + j, hi, lo, nk)

            for d in range(2):
                merge(d, d, False)
            with pe.Fori(1, KD // 2) as turn:
                d = turn * 2
                for par in range(2):
                    merge(d + par, par, True)
            for d in range(KD):
                if d == 0:
                    pe.wait_ge(tm_done, 2 * KD)
                unit(U_OUT + d, d % SLOTS, d, m_hi, m_lo, each_k=(m_lo_done, 0) if d == 0 else None)
            stats(3, 0, 1)
            stats(4, 4, 5)
            ffn(1, U_UP2)
            stats(5, 0, 1)
            for n in range(2 * TT):
                half, t = n // TT, n % TT
                for j in range(4):
                    k = 4 * half + j
                    if t == 0:
                        pe.wait_ge(x_ready, 2 * KD + k + 1)
                    mm = pe.transpose(ps[:, OUT_BANK[n], j * P:(j + 1) * P], xs[:, k, t * P:(t + 1) * P], c(IDENT))
                mm.then_inc(out_t, 1)

        @block.scalar
        def _(act_eng):
            act_eng.dma_start(cst[:, 0:CONST_COLS], const).then_inc(const_in, 16)
            for i, g in enumerate(gains):
                act_eng.dma_start(g_tok[i * KD:(i + 1) * KD, :], g.rearrange("(k p) -> k p", p=P)).then_inc(gains_in, 16)
            for t in range(TT):
                act_eng.dma_start(x_tok[:, t, :], x[t * P:(t + 1) * P, :]).then_inc(x_in[t], 16)
            act_eng.dma_start(decay[:, :, :], decay_t).then_inc(tables_in, 16)
            act_eng.dma_start(rope[:, :, :], rope_t).then_inc(tables_in, 16)

            def split(u, slot, turn, cols=UNIT):
                act_eng.wait_ge(raw_full[slot], turn * 16 + 16)
                wait(act_eng, unit_done, u - (SLOTS - 1))
                act_eng.activation(w_hi[:, slot, 0:cols], w_raw[:, slot, 0:cols], ACT.Copy).then_inc(w_hi_done, 1)

            def split_u(u):
                if u < U_END:
                    split(u, u % SLOTS, u // SLOTS, unit_cols(u))

            def squares(n, src, ready, r0):
                for k in range(KD):
                    act_eng.wait_ge(ready, r0 + k + 1)
                    wait(act_eng, sq_used, KD * n + k - 1)
                    act_eng.activation(sq[:, k % 2, :], src[:, k, :], ACT.Square).then_inc(sq_ready, 1)

            def root(n, s_bank):
                act_eng.wait_ge(sq_used, KD * (n + 1))
                act_eng.activation(std[:, :], ps[:, s_bank, 0:TT], ACT.Sqrt, bias=cst[:, EPS:EPS + 1],
                                   scale=1.0 / D).then_inc(std_ready, 1)

            def pre_norm(n, i, s_bank, ready, r0):
                squares(n, xs, ready, r0)
                root(n, s_bank)
                for k in range(KD):
                    act_eng.wait_ge(hf_ready, KD * i + k + 1)
                    act_eng.activation(h_hi[:, k, :], hf[:, k % 2, :], ACT.Copy).then_inc(h_hi_done, 1)

            def ffn(fi, u0):
                def step(f, j, turn):
                    for q in range(2):
                        v = 2 * j + q + AHEAD
                        split(f * 2 + u0 + q + AHEAD, v % SLOTS, turn + v // SLOTS)
                        if q == 0:
                            act_eng.wait_ge(unit_done, f * 2 + u0 + 1)
                            wait(act_eng, a_done, NF * fi + f - 1)
                            act_eng.activation(gate_s[:, j, :], ps[:, 2 * j, :], ACT.Silu).then_inc(silu_done, 1)

                def part(f, par):
                    act_eng.wait_ge(a_done, f + NF * fi + 1)
                    wait(act_eng, unit_done, f + u0 + 2 * NF - 1)
                    act_eng.activation(a_hi[:, par, :], act[:, f, :], ACT.Copy).then_inc(a_hi_done, 1)

                for j in range(2):
                    step(j, j, u0 // SLOTS)
                part0(fi)
                with act_eng.Fori(1, NF // 2) as i:
                    for j in range(2):
                        step(i * 2 + j, j, i + u0 // SLOTS)
                ud = u0 + 2 * NF
                split_u(ud + AHEAD)
                part(1, 1)
                with act_eng.Fori(0, (NF - 4) // SLOTS) as i:
                    for j in range(1, SLOTS + 1):
                        v = j + AHEAD
                        split(i * 4 + ud + v, v % SLOTS, i + ud // SLOTS + v // SLOTS)
                        part(i * 4 + j + 1, (j + 1) % 2)
                for f in range(NF - 3, NF):
                    split_u(ud + f + AHEAD)
                    if f + 1 < NF:
                        part(f + 1, (f + 1) % 2)

            def part0(fi):
                act_eng.wait_ge(a_done, NF * fi + 1)
                act_eng.activation(a_hi[:, 0, :], act[:, 0, :], ACT.Copy).then_inc(a_hi_done, 1)

            split_u(0)
            split_u(1)
            pre_norm(0, 0, 0, x_copied, 0)
            ffn(0, U_UP1)
            squares(1, ys, y_copied, 0)
            root(1, 0)
            pre_norm(2, 1, 4, x_ready, 0)

            for kind in range(2):
                for j in range(4):
                    split_u(U_V + 4 * kind + j + AHEAD)
                for t in (1, 3):
                    dst = v_sb if kind == 0 else v_r
                    if t < 3:
                        act_eng.wait_ge(v_ready, 3 * kind + t + 1)
                    else:
                        act_eng.wait_ge(unit_done, U_V + 4 * kind + 4)
                    act_eng.activation(dst[:, t, :], ps[:, 4 * kind + t, :], ACT.Copy).then_inc(v_copied, 1)

            act_eng.preload_act_table_set("natural_log_exp_and_others")
            nz = nl = nw = chain = 0
            for ev in events:
                if ev[0] == "mm" and ev[2] == 0:
                    split_u(U_HEADS + ev[1] + AHEAD)
                if ev[0] == "mm" and ev[2] == KD - 1:
                    f = ev[1]
                    s, j = f // 5, f % 5
                    act_eng_unit = U_HEADS + f + 1
                    if j < 2:
                        act_eng.wait_ge(unit_done, act_eng_unit)
                        if s >= 2:
                            act_eng.wait_ge(z_ready, 12 * (s - 2) + 8)
                        act_eng.activation(qk_hi[:, s % 2, j, :], ps[:, FILL + f % 2, :], ACT.Copy,
                                           scale=SBD ** -0.5 if j == 0 else 1.0).then_inc(q_hi_done, 1)
                    if j == 4:
                        act_eng.wait_ge(unit_done, act_eng_unit)
                        if s >= 2:
                            act_eng.wait_ge(gn_v, 3 * (s - 1))
                        act_eng.activation(g_r[:, s % 2, :], ps[:, FILL + f % 2, :], ACT.Copy).then_inc(g_copied, 1)
                elif ev[0] == "z":
                    p, hh, b = ev[1]
                    W = T - b * P
                    if hh < 2:
                        act_eng.wait_ge(z_ready, nz + 1)
                        wait(act_eng, sp_raw, nl - 1)
                        l = lt[:, nl % 2, 0:W]
                        act_eng.activation(l, ps[:, nz % 4, 0:W], ACT.Abs).then_inc(l_step, 1)
                        act_eng.wait_ge(l_step, 3 * nl + 1)
                        act_eng.activation(l, l, ACT.Exp, scale=-1.0).then_inc(l_step, 1)
                        act_eng.wait_ge(l_step, 3 * nl + 2)
                        act_eng.activation(l, l, ACT.Ln, bias=1.0).then_inc(l_step, 1)
                        nl += 1
                    nz += 1
                elif ev[0] == "s":
                    p, hh, b = ev[1]
                    W = T - b * P
                    zi = score_tiles.index(ev[1])
                    act_eng.wait_ge(s_done, nw + 1)
                    wait(act_eng, o_done, zi - 1)
                    act_eng.activation(wt[:, zi % 2, 0:W], ps[:, zi % 4, 0:W], ACT.Exp).then_inc(w_raw_done, 1)
                    nw += 1
                elif ev[0] == "sb_out":
                    p = ev[1]
                    act_eng.wait_ge(o_done, 12 * p + 8)
                    act_eng.activation(o_sb_hi[:, p, :], ps[:, O_SB, :], ACT.Copy).then_inc(osb_hi_done, 1)
                elif ev[0] == "gnA":
                    p = ev[1]
                    act_eng.wait_ge(o_done, 12 * (p + 1))
                    wait(act_eng, or_lo_done, p)
                    act_eng.activation(gn_t[:, :], ps[:, O_RET, :], ACT.Copy).then_inc(gn_copied, 1)
                elif ev[0] == "gnB":
                    act_eng.wait_ge(gn_centred, ev[1] + 1)
                    act_eng.activation(gn_t[:, :], gn_c[:, :], ACT.Square).then_inc(gn_squared, 1)
                elif ev[0] == "gnC":
                    p = ev[1]
                    act_eng.wait_ge(gn_var, p + 1)
                    act_eng.activation(gn_t[:, :], ps[:, O_RET, :], ACT.Sqrt, bias=cst[:, EPS + 1:EPS + 2]
                                       ).then_inc(gn_std, 1)
                    act_eng.wait_ge(g_copied, p + 1)
                    act_eng.activation(g_r[:, p % 2, :], g_r[:, p % 2, :], ACT.Silu).then_inc(gn_silu, 1)
                    act_eng.preload_act_table_set("natural_log_exp_and_others")
                elif ev[0] == "gnD":
                    p = ev[1]
                    act_eng.wait_ge(gn_v, 3 * p + 3)
                    act_eng.activation(o_r_hi[:, p, :], gn_t[:, :], ACT.Copy).then_inc(or_hi_done, 1)

            def merge(d, par, waits):
                for j in range(4):
                    v = j + AHEAD
                    split(d * 4 + U_MERGE + v, v % SLOTS, d + U_MERGE // SLOTS + v // SLOTS, half_units(v))
                    if j < 2:
                        act_eng.wait_ge(unit_done, d * 4 + U_MERGE + j + 1)
                        if waits:
                            act_eng.wait_ge(tm_done, d * 2 - 3 + j)
                        act_eng.activation(sig[:, 2 * par + j, :], ps[:, 4 * par + j, :], ACT.Sigmoid
                                           ).then_inc(sig_done, 1)
                act_eng.wait_ge(m_done, d + 1)
                act_eng.activation(m_hi[:, d, :], tm[:, par, 0, :], ACT.Copy).then_inc(m_hi_done, 1)

            for d in range(2):
                merge(d, d, False)
            with act_eng.Fori(1, KD // 2) as turn:
                d = turn * 2
                for par in range(2):
                    merge(d + par, par, True)
            for d in range(KD):
                split_u(U_OUT + d + AHEAD)
            squares(3, ys, y_copied, KD)
            root(3, 0)
            pre_norm(4, 2, 4, x_ready, KD)
            ffn(1, U_UP2)
            squares(5, ys, y_copied, 2 * KD)
            root(5, 0)
            for n in range(1, 2 * TT, 2):
                half, t = n // TT, n % TT
                act_eng.wait_ge(out_t, n + 1)
                act_eng.activation(x_tok[:, t, half * T:(half + 1) * T], ps[:, OUT_BANK[n], :], ACT.Copy
                                   ).then_inc(out_copied[1], 1)

        @block.vector
        def _(dve):
            def split(u, slot, cols=UNIT):
                dve.wait_ge(w_hi_done, u + 1)
                dve.tensor_tensor(w_lo[:, slot, 0:cols], w_raw[:, slot, 0:cols],
                                  w_hi[:, slot, 0:cols].bitcast(F32), ALU.subtract).then_inc(w_lo_done, 1)

            def split_u(u):
                if u < U_END:
                    split(u, u % SLOTS, unit_cols(u))

            def spread(n, factor):
                dve.wait_ge(std_ready, n + 1)
                dve.reciprocal(rstd[:, :], std[:, :]).then_inc(rstd_ready, 1)
                dve.wait_ge(rstd_ready, n + 1)
                for j in range(TT):
                    op = dve.tensor_scalar(diag[:, j, :], c(IDENT), rstd[:, j:j + 1], factor, ALU.mult, ALU.mult)
                op.then_inc(diag_ready, 1)
                dve.wait_ge(r_ready, n + 1)

            def pre_norm(n, i, r_bank, g):
                spread(n, 1.0)
                def lo(k):
                    dve.wait_ge(h_hi_done, KD * i + k + 1)
                    dve.tensor_tensor(h_lo[:, k, :], hf[:, k % 2, :], h_hi[:, k, :].bitcast(F32),
                                      ALU.subtract).then_inc(h_lo_done, 1)
                for k in range(KD):
                    if k >= 2:
                        dve.wait_ge(h_lo_done, KD * i + k - 1)
                    dve.scalar_tensor_tensor(out=hf[:, k % 2, :], in0=xs[:, k, :], scalar=gcol[:, g, k:k + 1],
                                             in1=ps[:, r_bank, :], op0=ALU.mult, op1=ALU.mult).then_inc(hf_ready, 1)
                    if k >= 1:
                        lo(k - 1)
                lo(KD - 1)

            def post_norm(n, i, r_bank, g, factor, ready):
                for k in range(KD):
                    ready(k)
                    dve.tensor_copy(ys[:, k, :], ps[:, k, :]).then_inc(y_copied, 1)
                spread(n, factor)
                for k in range(KD):
                    dve.wait_ge(y_copied, KD * i + k + 1)
                    dve.scalar_tensor_tensor(out=ys[:, k, :], in0=ys[:, k, :], scalar=gcol[:, g, k:k + 1],
                                             in1=ps[:, r_bank, :], op0=ALU.mult, op1=ALU.mult).then_inc(y_scaled, 1)

            def ffn(fi, u0):
                def step(f, j):
                    for q in range(2):
                        split(f * 2 + u0 + q + AHEAD, (2 * j + q + AHEAD) % SLOTS)
                    dve.wait_ge(silu_done, f + NF * fi + 1)
                    dve.wait_ge(unit_done, f * 2 + u0 + 2)
                    dve.tensor_tensor(act[:, f, :], gate_s[:, j, :], ps[:, 2 * j + 1, :], ALU.mult
                                      ).then_inc(a_done, 1)

                def part(f, par):
                    dve.wait_ge(a_hi_done, f + NF * fi + 1)
                    dve.tensor_tensor(a_lo[:, par, :], act[:, f, :], a_hi[:, par, :].bitcast(F32),
                                      ALU.subtract).then_inc(a_lo_done, 1)

                for j in range(2):
                    step(j, j)
                part(0, 0)
                with dve.Fori(1, NF // 2) as turn:
                    i = turn * 2
                    for j in range(2):
                        step(i + j, j)
                ud = u0 + 2 * NF
                split_u(ud + AHEAD)
                part(1, 1)
                with dve.Fori(0, (NF - 4) // SLOTS) as turn:
                    i = turn * SLOTS
                    for j in range(1, SLOTS + 1):
                        split(i + ud + j + AHEAD, (j + AHEAD) % SLOTS)
                        part(i + j + 1, (j + 1) % 2)
                for f in range(NF - 3, NF):
                    split_u(ud + f + AHEAD)
                    if f + 1 < NF:
                        part(f + 1, (f + 1) % 2)

            def ffn_out(fi, ud):
                def ready(k):
                    if k < KD - 1:
                        dve.wait_ge(y_ready, (KD - 1) * fi + k + 1)
                    else:
                        dve.wait_ge(unit_done, ud + NF)
                return ready

            dve.wait_ge(gains_t, 1)
            dve.tensor_copy(gcol[:, :, :].rearrange("p g k -> p (g k)"), ps[:, 0, 0:6 * KD]).then_inc(gains_ok, 1)
            split_u(0)
            split_u(1)
            for k in range(KD):
                dve.wait_ge(xt_done, k + 1)
                dve.tensor_copy(xs[:, k, :], ps[:, k, :]).then_inc(x_copied, 1)
            dve.wait_ge(gains_ok, 1)
            pre_norm(0, 0, 5, 0)
            ffn(0, U_UP1)
            post_norm(1, 0, 1, 1, 0.5, ffn_out(0, U_DOWN1))
            pre_norm(2, 1, 5, 2)

            for kind in range(2):
                for j in range(4):
                    split_u(U_V + 4 * kind + j + AHEAD)
                for t in (0, 2):
                    dst = v_sb if kind == 0 else v_r
                    dve.wait_ge(v_ready, 3 * kind + t + 1)
                    dve.tensor_copy(dst[:, t, :], ps[:, 4 * kind + t, :]).then_inc(v_copied, 1)

            dve.wait_ge(tables_in, 32)
            nz = nl = nret = nrope = 0
            for ev in events:
                if ev[0] == "mm" and ev[2] == 0:
                    split_u(U_HEADS + ev[1] + AHEAD)
                if ev[0] == "mm" and ev[2] == KD - 1:
                    f = ev[1]
                    s, j = f // 5, f % 5
                    bank = ps[:, FILL + f % 2, :]
                    if j < 2:
                        dve.wait_ge(q_hi_done, 2 * s + j + 1)
                        dve.scalar_tensor_tensor(out=qk_lo[:, s % 2, j, :], in0=bank,
                                                 scalar=SBD ** -0.5 if j == 0 else 1.0,
                                                 in1=qk_hi[:, s % 2, j, :].bitcast(F32), op0=ALU.mult,
                                                 op1=ALU.subtract).then_inc(q_lo_done, 1)
                    elif j < 4:
                        dve.wait_ge(unit_done, U_HEADS + f + 1)
                        wait(dve, rope_done, nrope)
                        if s >= 2:
                            dve.wait_ge(z_ready, 12 * (s - 1))
                        lo, hi = slice(0, RD // 2), slice(RD // 2, RD)
                        dve.tensor_tensor(qk_r[:, s % 2, j - 2, :], bank, rope[:, 0, :], ALU.mult).then_inc(rope_mul, 1)
                        dve.tensor_tensor(ropeB[lo, :], ps[hi, FILL + f % 2, :], rope[hi, 1, :], ALU.mult
                                          ).then_inc(rope_mul, 1)
                        dve.tensor_tensor(ropeB[hi, :], ps[lo, FILL + f % 2, :], rope[lo, 1, :], ALU.mult
                                          ).then_inc(rope_mul, 1)
                        nrope += 1
                elif ev[0] == "z":
                    p, hh, b = ev[1]
                    W = T - b * P
                    if hh < 2:
                        dve.wait_ge(l_step, 3 * nl + 3)
                        wait(dve, s_done, nl - 1)
                        wait(dve, cum_done, 3 * ((nl - 1) // 4) + min((nl - 1) % 4, 3) if nl >= 2 else 0)
                        dve.scalar_tensor_tensor(out=sp[:, nl % 2, 0:W], in0=ps[:, nz % 4, 0:W], scalar=0.0,
                                                 in1=lt[:, nl % 2, 0:W], op0=ALU.max, op1=ALU.add
                                                 ).then_inc(sp_raw, 1)
                        nl += 1
                    else:
                        dve.wait_ge(z_ready, nz + 1)
                        wait(dve, o_done, nz - 1)
                        dve.tensor_tensor(wt[:, nz % 2, 0:W], ps[:, nz % 4, 0:W], decay[:, p, 0:W], ALU.mult
                                          ).then_inc(w_ret, 1)
                        nret += 1
                    nz += 1
                elif ev[0] == "sb_out":
                    p = ev[1]
                    dve.wait_ge(osb_hi_done, p + 1)
                    dve.tensor_tensor(o_sb_lo[:, p, :], ps[:, O_SB, :], o_sb_hi[:, p, :].bitcast(F32), ALU.subtract
                                      ).then_inc(osb_lo_done, 1)
                elif ev[0] == "gnB":
                    p = ev[1]
                    dve.wait_ge(gn_mean, p + 1)
                    dve.tensor_tensor(gn_c[:, :], gn_t[:, :], ps[:, O_RET, :], ALU.subtract).then_inc(gn_centred, 1)
                elif ev[0] == "gnC":
                    p = ev[1]
                    dve.wait_ge(gn_std, p + 1)
                    dve.reciprocal(gn_t[:, :], gn_t[:, :]).then_inc(gn_v, 1)
                    dve.wait_ge(gn_v, 3 * p + 1)
                    dve.tensor_tensor(gn_c[:, :], gn_c[:, :], gn_t[:, :], ALU.mult).then_inc(gn_v, 1)
                    dve.wait_ge(gn_v, 3 * p + 2)
                    dve.wait_ge(gn_silu, p + 1)
                    dve.tensor_tensor(gn_t[:, :], gn_c[:, :], g_r[:, p % 2, :], ALU.mult).then_inc(gn_v, 1)
                elif ev[0] == "gnD":
                    p = ev[1]
                    dve.wait_ge(or_hi_done, p + 1)
                    dve.tensor_tensor(o_r_lo[:, p, :], gn_t[:, :], o_r_hi[:, p, :].bitcast(F32), ALU.subtract
                                      ).then_inc(or_lo_done, 1)

            def merge(d, par, waits):
                for j in range(4):
                    v = j + AHEAD
                    split(d * 4 + U_MERGE + v, v % SLOTS, half_units(v))
                    if j >= 2:
                        dve.wait_ge(unit_done, d * 4 + U_MERGE + j + 1)
                        dve.wait_ge(sig_done, d * 2 + j - 1)
                        if waits and j == 2:
                            dve.wait_ge(m_lo_done, d - 1)
                        dve.tensor_tensor(tm[:, par, j - 2, :], sig[:, 2 * par + j - 2, :], ps[:, 4 * par + j, :],
                                          ALU.mult).then_inc(tm_done, 1)
                dve.wait_ge(tm_done, d * 2 + 2)
                dve.tensor_tensor(tm[:, par, 0, :], tm[:, par, 0, :], tm[:, par, 1, :], ALU.add).then_inc(m_done, 1)
                dve.wait_ge(m_hi_done, d + 1)
                dve.tensor_tensor(m_lo[:, d, :], tm[:, par, 0, :], m_hi[:, d, :].bitcast(F32), ALU.subtract
                                  ).then_inc(m_lo_done, 1)

            for d in range(2):
                merge(d, d, False)
            with dve.Fori(1, KD // 2) as turn:
                d = turn * 2
                for par in range(2):
                    merge(d + par, par, True)

            def out_ready(k):
                split_u(U_OUT + k + AHEAD)
                dve.wait_ge(unit_done, U_OUT + k + 1)
            post_norm(3, 1, 1, 3, 1.0, out_ready)
            pre_norm(4, 2, 5, 4)
            ffn(1, U_UP2)
            post_norm(5, 2, 1, 5, 0.5, ffn_out(1, U_DOWN2))
            for n in range(0, 2 * TT, 2):
                half, t = n // TT, n % TT
                dve.wait_ge(out_t, n + 1)
                dve.tensor_copy(x_tok[:, t, half * T:(half + 1) * T], ps[:, OUT_BANK[n], :]).then_inc(out_copied[0], 1)

        @block.gpsimd
        def _(pool):
            def residual(i):
                for k in range(KD):
                    pool.wait_ge(y_scaled, KD * i + k + 1)
                    pool.tensor_tensor(xs[:, k, :], xs[:, k, :], ys[:, k, :], ALU.add).then_inc(x_ready, 1)

            residual(0)
            nl = nw = nrope = 0
            for ev in events:
                if ev[0] == "mm" and ev[2] == KD - 1 and ev[1] % 5 in (2, 3):
                    s, j = ev[1] // 5, ev[1] % 5 - 2
                    pool.wait_ge(rope_mul, 3 * nrope + 3)
                    pool.tensor_tensor(qk_r[:, s % 2, j, :], qk_r[:, s % 2, j, :], ropeB[:, :], ALU.add
                                       ).then_inc(rope_done, 1)
                    nrope += 1
                elif ev[0] == "z" and ev[1][1] < 2:
                    b = ev[1][2]
                    pool.wait_ge(sp_raw, nl + 1)
                    pool.affine_select(out=sp[:, nl % 2, 0:P], in_=sp[:, nl % 2, 0:P], pattern=[[1, P]],
                                       compare_op=ALU.is_gt, fill=0.0, base=0, channel_multiplier=-1
                                       ).then_inc(sp_ready, 1)
                    if b > 0:
                        pool.wait_ge(sp_ready, nl + 1)
                        wait(pool, s_done, nl)
                        wait(pool, cum_done, 3 * (nl // 4) + TT - 1 - b)
                        new = cum[:, b % 2, :]
                        if b == TT - 1:
                            pool.tensor_copy(new[:, (b - 1) * P:b * P], sp[:, nl % 2, 0:P]).then_inc(cum_done, 1)
                        else:
                            pool.tensor_copy(new[:, (b - 1) * P:b * P], sp[:, nl % 2, 0:P])
                            pool.tensor_tensor(new[:, b * P:T - P], cum[:, (b + 1) % 2, b * P:T - P],
                                               sp[:, nl % 2, P:T - b * P], ALU.add).then_inc(cum_done, 1)
                    nl += 1
                elif ev[0] == "s":
                    zi = score_tiles.index(ev[1])
                    pool.wait_ge(w_raw_done, nw + 1)
                    pool.affine_select(out=wt[:, zi % 2, 0:P], in_=wt[:, zi % 2, 0:P], pattern=[[1, P]],
                                       compare_op=ALU.is_gt, fill=0.0, base=0, channel_multiplier=-1
                                       ).then_inc(w_masked, 1)
                    nw += 1
            residual(1)
            residual(2)


_WEIGHTS = ("w_ffn1_gate", "w_ffn1_up", "w_ffn1_down", "w_in", "w_proj_sb", "w_proj_ret", "w_out",
            "w_ffn2_gate", "w_ffn2_up", "w_ffn2_down")
_GAINS = ("g_ffn1_pre", "g_ffn1_post", "g_mix_pre", "g_mix_post", "g_ffn2_pre", "g_ffn2_post")


def kernel(**inputs):
    import concourse.bacc as bacc
    from concourse.bass_utils import run_bass_kernel_spmd

    nc = bacc.Bacc("TRN2", target_bir_lowering=False, num_devices=1)
    arrays, aps = {}, {}

    def give(name, a):
        a = np.ascontiguousarray(a)
        arrays[name] = a
        aps[name] = nc.dram_tensor(name, a.shape, F32, kind="ExternalInput").ap()

    for name in ("x", *_WEIGHTS, *_GAINS):
        give(name, np.asarray(inputs[name])[0])
    for name, table in zip(("const", "decay_t", "rope_t"), constants()):
        give(name, table)
    out = nc.dram_tensor("out", (T, D), F32, kind="ExternalOutput").ap()
    build(nc, aps["x"], [aps[g] for g in _GAINS], *[aps[w] for w in _WEIGHTS],
          aps["const"], aps["decay_t"], aps["rope_t"], out)
    r = run_bass_kernel_spmd(nc, [arrays], core_ids=[0])
    return r.results[0]["out"].reshape(1, T, D)
```

```python
from contextlib import ExitStack

import numpy as np

import concourse.bass as bass
from concourse import mybir

ALU = mybir.AluOpType
ACT = mybir.ActivationFunctionType
F32 = mybir.dt.float32
F32R = mybir.dt.float32r

P = 128
T = 512
D = 1024
KD = D // P
TT = T // P
FF = 4096
NF = FF // P
SBH, SBD = 8, 64
RH, RD = 4, 128
PAIRS = SBH * SBD // P
RMS_EPS, GN_EPS = 1e-6, 1e-5
ARENA = 212832
UNIT = KD * P
SLOTS = 4
AHEAD = 2

U_UP1 = 0
U_DOWN1 = U_UP1 + 2 * NF
U_V = U_DOWN1 + NF
U_HEADS = U_V + 8
U_MERGE = U_HEADS + 5 * PAIRS
U_OUT = U_MERGE + 4 * KD
U_UP2 = U_OUT + KD
U_DOWN2 = U_UP2 + 2 * NF
U_END = U_DOWN2 + NF

C_QSB, C_KSB, C_VSB, C_QR, C_KR, C_VR, C_GR, C_GATE_SB, C_GATE_RET = 0, 4, 8, 12, 16, 20, 24, 28, 36

IDENT, ONES, MEAN, NEG_TRI, NEG_ONES, EPS = 0, 128, 256, 384, 512, 640
CONST_COLS = 642


def constants():
    p = np.arange(P)
    c = np.zeros((P, CONST_COLS), np.float32)
    c[:, IDENT:IDENT + P] = np.eye(P)
    c[:, ONES:ONES + P] = 1.0
    c[:, MEAN:MEAN + P] = 1.0 / RD
    c[:, NEG_TRI:NEG_TRI + P] = np.where(p[:, None] >= p[None, :], -1.0, 0.0)
    c[:, NEG_ONES:NEG_ONES + P] = -1.0
    c[:, EPS] = RMS_EPS
    c[:, EPS + 1] = GN_EPS
    log_gamma = np.log(1.0 - 2.0 ** (-5.0 - np.arange(RH)))
    lag = np.arange(T)[None, :] - p[:, None]
    decay = np.where(lag[:, None] >= 0, np.exp(np.maximum(lag, 0)[:, None] * log_gamma[None, :, None]), 0.0)
    decay = (decay * RD ** -0.5).astype(np.float32)
    half = RD // 2
    inv = (np.float32(10000.0) ** (-np.arange(half, dtype=np.float32) / np.float32(half))).astype(np.float32)
    ang = (np.arange(T, dtype=np.float32)[None, :] * inv[:, None]).astype(np.float32)
    cos, sin = np.cos(ang.astype(np.float64)), np.sin(ang.astype(np.float64))
    rope = np.stack([np.concatenate([cos, cos]), np.concatenate([sin, -sin])], 1).astype(np.float32)
    return c, decay, rope


FILLS = [("q", 0), ("k", 0)]
for _p in range(PAIRS):
    FILLS += [("qr", _p), ("kr", _p)] + ([("q", _p + 1), ("k", _p + 1)] if _p + 1 < PAIRS else []) + [("g", _p)]
FILL_COL = {"q": C_QSB, "k": C_KSB, "qr": C_QR, "kr": C_KR, "g": C_GR}


def schedule_heads():
    tiles = [(p, hh, b) for p in range(PAIRS) for hh in range(3) for b in reversed(range(TT))]
    fill = [("mm", f, k) for f in range(len(FILLS)) for k in range(KD)]
    fill += [("gate", j, k) for j in range(2) for k in range(KD)]
    per_pair = 12
    gn_at = {4: "a", 5: "b", 6: "c", 7: "d", 8: "e", 10: "f"}
    groups = []
    for n in range(len(tiles) + 12):
        group = []
        if n < len(tiles):
            group.append(("z", tiles[n]))
        if 2 <= n < len(tiles) + 2 and tiles[n - 2][1] < 2:
            group.append(("s", tiles[n - 2]))
        if 4 <= n < len(tiles) + 4:
            group.append(("o", tiles[n - 4]))
        p, r = n // per_pair, n % per_pair
        if r == 11 and p < PAIRS:
            group.append(("sb_out", p))
        if p >= 1 and r in gn_at:
            group.append(("gn_" + gn_at[r], p - 1))
        groups.append(group)
    lead, last = 2 * KD + 4, per_pair * PAIRS - 6
    need = (len(FILLS) - 1) * KD
    events, at = fill[:lead], lead
    for n, group in enumerate(groups):
        events += group
        upto = lead + (need - lead) * (n + 1) // last if n < last else (
            need + (len(fill) - need) * (n + 1 - last) // (len(groups) - last))
        events += fill[at:upto]
        at = upto
    return events


def build(nc, x, gains, w_gate1, w_up1, w_down1, w_in, w_proj_sb, w_proj_ret, w_out,
          w_gate2, w_up2, w_down2, const, decay_t, rope_t, out):
    with ExitStack() as ctx:
        base = -(-nc.sbuf_base // 32) * 32
        ctx.enter_context(nc.sbuf_tensor("arena", [P, ARENA // 4], F32))
        top = [0]

        def place(name, shape, dt=F32, at=None):
            size = -(-int(np.prod(shape[1:])) * 4 // 32) * 32
            off = top[0] if at is None else at
            if at is None:
                top[0] += size
            assert off + size <= ARENA, (name, off + size)
            return nc.alloc_sbuf_tensor_at(name, shape, dt, offset=base + off), off + size

        xs, _ = place("xs", [P, KD, T])
        h_hi, _ = place("h_hi", [P, KD, T], F32R)
        h_lo, _ = place("h_lo", [P, KD, T], F32R)
        w_raw, _ = place("w_raw", [P, SLOTS, UNIT])
        w_hi, _ = place("w_hi", [P, SLOTS, UNIT], F32R)
        w_lo, _ = place("w_lo", [P, SLOTS, UNIT], F32R)
        cst, _ = place("cst", [P, CONST_COLS])
        gcol, _ = place("gcol", [P, 6, KD])
        std, _ = place("std", [P, TT])
        rstd, _ = place("rstd", [P, TT])
        r_tok, _ = place("r_tok", [P, TT])
        r_tok2, _ = place("r_tok2", [P, TT])
        ms, _ = place("ms", [P, TT])
        r_all, _ = place("r_all", [P, T])
        decay, _ = place("decay", [P, RH, T])
        rope, _ = place("rope", [P, 2, T])
        region = top[0]
        act, e = place("act", [P, NF, T], at=region)
        a_hi, e = place("a_hi", [P, 2, T], F32R, at=e)
        a_lo, e = place("a_lo", [P, 2, T], F32R, at=e)
        gate_s, e = place("gate_s", [P, 2, T], at=e)
        ys, e2 = place("ys", [P, KD, T], at=region)
        sq, e2 = place("sq", [P, 3, T], at=e2)
        acc, e2 = place("acc", [P, T], at=e2)
        diag, e2 = place("diag", [P, TT, P], at=e2)
        x_tok, _ = place("x_tok", [P, TT, D], at=e2)
        g_tok, _ = place("g_tok", [6 * KD, P], at=e)
        v_sb, e3 = place("v_sb", [P, TT, T], at=region)
        v_r, e3 = place("v_r", [P, TT, T], at=e3)
        qk_hi, e3 = place("qk_hi", [P, 2, 2, T], F32R, at=e3)
        qk_lo, e3 = place("qk_lo", [P, 2, 2, T], F32R, at=e3)
        qk_r, e3 = place("qk_r", [P, 2, T], at=e3)
        g_r, e3 = place("g_r", [P, T], at=e3)
        sp, e3 = place("sp", [P, 3, T], at=e3)
        cum, e3 = place("cum", [P, 3, T - P], at=e3)
        wt, e3 = place("wt", [P, 4, T], at=e3)
        proj_t, e3 = place("proj_t", [P, T], at=e3)
        gn_c, e3 = place("gn_c", [P, T], at=e3)
        gn_t, e3 = place("gn_t", [P, T], at=e3)
        oe = ARENA - 4 * PAIRS * T * 4
        assert e3 <= oe
        o_sb_hi, e4 = place("o_sb_hi", [P, PAIRS, T], F32R, at=oe)
        o_sb_lo, e4 = place("o_sb_lo", [P, PAIRS, T], F32R, at=e4)
        o_r_hi, e4 = place("o_r_hi", [P, RH, T], F32R, at=e4)
        o_r_lo, e4 = place("o_r_lo", [P, RH, T], F32R, at=e4)
        me = e2
        m_hi, e5 = place("m_hi", [P, KD, T], F32R, at=me)
        m_lo, e5 = place("m_lo", [P, KD, T], F32R, at=e5)
        assert e5 <= oe, (e5, oe)
        sig, e6 = place("sig", [P, 4, T], at=region)
        tm, e6 = place("tm", [P, 2, 2, T], at=e6)
        assert e6 <= me

        ps = ctx.enter_context(nc.psum_tensor("ps", [P, 8, T], F32))

        def sem(name):
            return ctx.enter_context(nc.semaphore(name))

        raw_full = [sem(f"raw_full{i}") for i in range(SLOTS)]
        w_hi_done, w_lo_done, unit_done = sem("w_hi_done"), sem("w_lo_done"), sem("unit_done")
        const_in, gains_in, tables_in = sem("const_in"), sem("gains_in"), sem("tables_in")
        x_in = [sem(f"x_in{t}") for t in range(TT)]
        gains_t, gains_ok = sem("gains_t"), sem("gains_ok")
        xt_done, x_copied = sem("xt_done"), [sem("x_copied_v"), sem("x_copied_s")]
        gate_scaled, silu_done, a_done, a_hi_done, a_lo_done = (
            sem("gate_scaled"), sem("silu_done"), sem("a_done"), sem("a_hi_done"), sem("a_lo_done"))
        y_ready, y_kept, ysq_ready, yacc_done, y_scaled = (
            sem("y_ready"), sem("y_kept"), sem("ysq_ready"), sem("yacc_done"), sem("y_scaled"))
        stat_done, ms_ready, std_ready, rstd_ready = sem("stat_done"), sem("ms_ready"), sem("std_ready"), sem("rstd_ready")
        diag_ready, r_ready, r_all_ready = sem("diag_ready"), sem("r_ready"), sem("r_all_ready")
        x_ready, x_ready_v = sem("x_ready"), sem("x_ready_v")
        h_hi_done, h_lo_done = sem("h_hi_done"), sem("h_lo_done")
        xsq_ready, xacc_p, xacc_v = sem("xsq_ready"), sem("xacc_p"), sem("xacc_v")
        v_ready, v_copied = sem("v_ready"), sem("v_copied")
        q_scaled, rope_scaled, q_hi_done, q_lo_done, rope_mul, rope_done, g_copied = (
            sem("q_scaled"), sem("rope_scaled"), sem("q_hi_done"), sem("q_lo_done"), sem("rope_mul"), sem("rope_done"), sem("g_copied"))
        z_ready, l_step, sp_raw, sp_ready, cum_done, s_done = (
            sem("z_ready"), sem("l_step"), sem("sp_raw"), sem("sp_ready"), sem("cum_done"), sem("s_done"))
        w_raw_done, w_masked, w_ret, o_done = sem("w_raw_done"), sem("w_masked"), sem("w_ret"), sem("o_done")
        osb_hi_done, osb_lo_done = sem("osb_hi_done"), sem("osb_lo_done")
        gn_copied, gn_mean, gn_centred, gn_squared, gn_var, gn_std, gn_silu = (
            sem("gn_copied"), sem("gn_mean"), sem("gn_centred"), sem("gn_squared"), sem("gn_var"), sem("gn_std"),
            sem("gn_silu"))
        gn_v, or_hi_done, or_lo_done = sem("gn_v"), sem("or_hi_done"), sem("or_lo_done")
        branch_scaled, sig_done, tm_done, m_done, m_hi_done, m_lo_done = (
            sem("branch_scaled"), sem("sig_done"), sem("tm_done"), sem("m_done"), sem("m_hi_done"), sem("m_lo_done"))
        out_t, out_stored = sem("out_t"), sem("out_stored")
        out_copied = [sem("out_copied_v"), sem("out_copied_s")]

        def wait(eng, s, value):
            if isinstance(value, int) and value <= 0:
                return
            eng.wait_ge(s, value)

        def cum_count(i):
            return 3 * (i // 4) + min(i % 4 + 1, 3) if i >= 0 else 0

        def c(col, n=P):
            return cst[:, col:col + n]

        events = schedule_heads()
        score_tiles = [e[1] for e in events if e[0] == "z"]
        sb_tiles = [t for t in score_tiles if t[1] < 2]
        ret_tiles = [t for t in score_tiles if t[1] == 2]
        o_tiles = [e[1] for e in events if e[0] == "o"]
        s_tiles = [e[1] for e in events if e[0] == "s"]
        assert o_tiles == score_tiles and s_tiles == sb_tiles

        R_POST, R_PRE = 4, 5
        Y_ORDER = (R_POST, 0, 1, 2, 3, 5, 6, 7)
        O_SB, O_RET, FILL = 4, 5, 6
        GATE_BANK = (6, 7)

        def merge_bank(par, j):
            return ((6, 7, 0, 1), (2, 3, 4, 5))[par][j]

        def half_units(stage_unit):
            return UNIT // 2 if stage_unit % 4 >= 2 else UNIT

        def unit_cols(u):
            return half_units(u - U_MERGE) if U_MERGE <= u < U_OUT else UNIT

        block = ctx.enter_context(nc.Block())

        @block.sync
        def _(sp_eng):
            def load(u, slot, src, cols=UNIT):
                wait(sp_eng, w_lo_done, u - (SLOTS - 1))
                dst = w_raw[:, slot, 0:cols].rearrange("p (k c) -> p k c", k=src.shape[1])
                sp_eng.dma_start(dst, src).then_inc(raw_full[slot], 16)

            def cols(w, f):
                return w.rearrange("(k p) c -> p k c", p=P)[:, :, bass.ts(f, P)]

            def ffn_loads(u0, wg, wu, wd):
                def up(i):
                    for j in range(2):
                        load(i * 2 + u0 + 2 * j, 2 * j, cols(wg, i + j))
                        load(i * 2 + u0 + 2 * j + 1, 2 * j + 1, cols(wu, i + j))

                def down(i):
                    for j in range(SLOTS):
                        load(i + u0 + 2 * NF + j, j, wd[bass.ts(i + j, P), :].rearrange("p (k c) -> p k c", k=KD))

                up(0)
                with sp_eng.Fori(1, NF // 2) as turn:
                    i = turn * 2
                    up(i)
                with sp_eng.Fori(0, NF // SLOTS) as turn:
                    i = turn * SLOTS
                    down(i)

            for t in (1, 3):
                sp_eng.dma_start(x_tok[:, t, :], x[t * P:(t + 1) * P, :]).then_inc(x_in[t], 16)
            ffn_loads(U_UP1, w_gate1, w_up1, w_down1)
            u = U_V
            for c0 in (C_VSB, C_VR):
                for j in range(4):
                    src = w_in[2 * j * P:(2 * j + 2) * P, c0 * P:c0 * P + T].rearrange("(k p) c -> p k c", p=P)
                    load(u, u % SLOTS, src)
                    u += 1
            for kind, p in FILLS:
                load(u, u % SLOTS, cols(w_in, FILL_COL[kind] + p))
                u += 1
            with sp_eng.Fori(0, KD) as d:
                load(d * 4 + U_MERGE, 0, cols(w_in, d + C_GATE_SB))
                load(d * 4 + U_MERGE + 1, 1, cols(w_in, d + C_GATE_RET))
                load(d * 4 + U_MERGE + 2, 2, cols(w_proj_sb, d), UNIT // 2)
                load(d * 4 + U_MERGE + 3, 3, cols(w_proj_ret, d), UNIT // 2)
            for d in range(KD):
                load(U_OUT + d, d % SLOTS, cols(w_out, d))
            ffn_loads(U_UP2, w_gate2, w_up2, w_down2)
            for n in range(2 * TT):
                half, t = n // TT, n % TT
                sp_eng.wait_ge(out_copied[n % 2], n // 2 + 1)
                sp_eng.dma_start(out[t * P:(t + 1) * P, half * T:(half + 1) * T],
                                 x_tok[:, t, half * T:(half + 1) * T]).then_inc(out_stored, 16)
            sp_eng.wait_ge(out_stored, 16 * 2 * TT)

        @block.tensor
        def _(pe):
            def evacuated(f):
                kind, p = FILLS[f]
                if kind in ("q", "k"):
                    pe.wait_ge(q_scaled, 2 * p + "qk".index(kind) + 1)
                elif kind in ("qr", "kr"):
                    pe.wait_ge(rope_mul, 3 * (2 * p + ("qr", "kr").index(kind)) + 3)
                else:
                    pe.wait_ge(g_copied, p + 1)

            def bank_read(i):
                tile = score_tiles[i]
                if tile[1] < 2:
                    pe.wait_ge(w_raw_done, sb_tiles.index(tile) + 1)
                else:
                    pe.wait_ge(w_ret, ret_tiles.index(tile) + 1)

            def product(bank, w_at, src_hi, src_lo, first, last, m=slice(None)):
                (slot, col) = w_at
                wh, wl = w_hi[:, slot, col:col + P], w_lo[:, slot, col:col + P]
                pe.matmul(ps[:, bank, :], wh, src_hi, start=first, stop=False)
                pe.matmul(ps[:, bank, :], wh, src_lo, start=False, stop=False)
                return pe.matmul(ps[:, bank, :], wl, src_hi, start=False, stop=last)

            def unit(u, slot, bank, hi, lo, nk=KD, each_k=None, midway=None):
                pe.wait_ge(w_lo_done, u + 1)
                for k in range(nk):
                    if each_k is not None:
                        pe.wait_ge(each_k[0], each_k[1] + k + 1)
                    if midway is not None and k == nk // 2:
                        midway()
                    last = product(bank, (slot, k * P), hi[:, k, :], lo[:, k, :], k == 0, k == nk - 1)
                last.then_inc(unit_done, 1)

            def token_sums(bank, squares, first, last):
                for j in range(TT):
                    mm = pe.matmul(ps[:, bank, j:j + 1], squares[:, j * P:(j + 1) * P], c(ONES, 1),
                                   start=(first and j == 0), stop=last, skip_group_check=True)
                return mm

            def spread(n, bank):
                pe.wait_ge(diag_ready, n + 1)
                pe.matmul(ps[:, bank, :], c(ONES), diag[:, :, :].rearrange("p j t -> p (j t)"),
                          start=True, stop=True).then_inc(r_ready, 1)

            def post_stats(i):
                pe.wait_ge(y_kept, i + 1)
                pe.wait_ge(yacc_done, 6 * (i + 1))
                token_sums(R_POST, acc[:, :], True, False)
                pe.wait_ge(ysq_ready, KD * (i + 1))
                token_sums(R_POST, sq[:, (KD - 1) % 3, :], False, True).then_inc(stat_done, 1)
                spread(2 * i + 1, R_POST)

            def pre_sums(i):
                pe.wait_ge(xacc_v, 4 * (i + 1))
                token_sums(R_PRE, ys[:, 1, :], True, True).then_inc(stat_done, 1)

            def ffn(fi, u0):
                def up(i, j):
                    f = i + j
                    wait(pe, gate_scaled, f + NF * fi - 1)
                    unit(f * 2 + u0, 2 * j, 2 * j, h_hi, h_lo)
                    wait(pe, a_done, f + NF * fi - 1)
                    unit(f * 2 + u0 + 1, 2 * j + 1, 2 * j + 1, h_hi, h_lo)

                pe.wait_ge(w_lo_done, u0 + 2)
                wait(pe, r_all_ready, 4 * fi)
                for k in range(KD):
                    pe.wait_ge(h_lo_done, 2 * KD * fi + k + 1)
                    for j in range(2):
                        mm = product(j, (j, k * P), h_hi[:, k, :], h_lo[:, k, :], k == 0, k == KD - 1)
                        if k == KD - 1:
                            mm.then_inc(unit_done, 1)
                unit(u0 + 2, 2, 2, h_hi, h_lo)
                pre_sums(2 * fi)
                unit(u0 + 3, 3, 3, h_hi, h_lo, midway=lambda: spread(4 * fi, R_PRE))
                with pe.Fori(1, NF // 2) as turn:
                    i = turn * 2
                    for j in range(2):
                        up(i, j)

                def down(f, slot, banks, first=False, last=False):
                    pe.wait_ge(w_lo_done, f + u0 + 2 * NF + 1)
                    pe.wait_ge(a_lo_done, f + NF * fi + 1)
                    for d in banks:
                        if first and d == 0:
                            pe.wait_ge(a_done, NF * (fi + 1))
                        par = slot % 2
                        mm = product(d, (slot, d * P), a_hi[:, par, :], a_lo[:, par, :], first, last)
                        if last and d != banks[-1]:
                            mm.then_inc(y_ready, 1)
                    mm.then_inc(unit_done, 1)

                pe.wait_ge(r_all_ready, 4 * fi + 1)
                down(0, 0, (4, 5, 6, 7, 0, 1, 2, 3), first=True)
                with pe.Fori(0, (NF - 3) // SLOTS) as turn:
                    i = turn * SLOTS + 1
                    for j in range(SLOTS):
                        down(i + j, (j + 1) % SLOTS, range(KD))
                for f in range(NF - 3, NF):
                    down(f, f % SLOTS, Y_ORDER, last=(f == NF - 1))

            pe.wait_ge(const_in, 16)
            pe.wait_ge(gains_in, 16 * 6)
            pe.transpose(ps[:, 0, 0:6 * KD], g_tok[:, :], cst[0:6 * KD, IDENT:IDENT + 6 * KD]).then_inc(gains_t, 1)
            pe.wait_ge(gains_ok, 1)
            for k in range(KD):
                for t in range(TT):
                    if k == 0:
                        pe.wait_ge(x_in[t], 16)
                    mm = pe.transpose(ps[:, k, t * P:(t + 1) * P], x_tok[:, t, k * P:(k + 1) * P], c(IDENT))
                mm.then_inc(xt_done, 1)
            ffn(0, U_UP1)
            post_stats(0)

            for kind in range(2):
                for j in range(4):
                    u = U_V + 4 * kind + j
                    pe.wait_ge(w_lo_done, u + 1)
                    for kk in range(2):
                        k = 2 * j + kk
                        if kind == 0:
                            pe.wait_ge(h_lo_done, KD + k + 1)
                        if kind == 0 and k == KD - 2:
                            pre_sums(1)
                        if kind == 0 and k == KD - 1:
                            spread(2, R_PRE)
                        for t in range(TT):
                            tok = slice(t * P, (t + 1) * P)
                            wc = slice(kk * T, (kk + 1) * T)
                            bank = ps[:, 4 * kind + t, :]
                            if k == 0 and 4 * kind + t == R_PRE:
                                pe.wait_ge(r_all_ready, 3)
                            pe.matmul(bank, h_hi[:, k, tok], w_hi[:, u % SLOTS, wc], start=(k == 0), stop=False)
                            pe.matmul(bank, h_hi[:, k, tok], w_lo[:, u % SLOTS, wc], start=False, stop=False)
                            mm = pe.matmul(bank, h_lo[:, k, tok], w_hi[:, u % SLOTS, wc], start=False,
                                           stop=(k == KD - 1))
                            if k == KD - 1 and t < TT - 1:
                                mm.then_inc(v_ready, 1)
                    mm.then_inc(unit_done, 1)

            nz = ns = no = 0
            for ev in events:
                if ev[0] == "mm":
                    f, k = ev[1], ev[2]
                    u = U_HEADS + f
                    if k == 0:
                        pe.wait_ge(w_lo_done, u + 1)
                        if f < 2:
                            pe.wait_ge(v_copied, 8)
                        else:
                            evacuated(f - 2)
                    mm = product(FILL + f % 2, (u % SLOTS, k * P), h_hi[:, k, :], h_lo[:, k, :],
                                 k == 0, k == KD - 1)
                    if k == KD - 1:
                        mm.then_inc(unit_done, 1)
                elif ev[0] == "z":
                    p, hh, b = ev[1]
                    W = T - b * P
                    if b == TT - 1 and hh == 0:
                        pe.wait_ge(q_lo_done, 2 * p + 2)
                    if b == TT - 1 and hh == 2:
                        pe.wait_ge(rope_done, 2 * p + 2)
                    if nz >= 4:
                        bank_read(nz - 4)
                    bank = ps[:, nz % 4, 0:W]
                    keys, queries = slice(b * P, (b + 1) * P), slice(b * P, T)
                    if hh < 2:
                        r = slice(hh * SBD, (hh + 1) * SBD)
                        q_h, q_l = qk_hi[r, p % 2, 0, queries], qk_lo[r, p % 2, 0, queries]
                        k_h, k_l = qk_hi[r, p % 2, 1, keys], qk_lo[r, p % 2, 1, keys]
                        pe.matmul(bank, k_h, q_h, start=True, stop=False)
                        pe.matmul(bank, k_h, q_l, start=False, stop=False)
                        mm = pe.matmul(bank, k_l, q_h, start=False, stop=True)
                    else:
                        mm = pe.matmul(bank, qk_r[:, 1, keys], qk_r[:, 0, queries], start=True, stop=True)
                    mm.then_inc(z_ready, 1)
                    nz += 1
                elif ev[0] == "s":
                    p, hh, b = ev[1]
                    W = T - b * P
                    zi = score_tiles.index(ev[1])
                    pe.wait_ge(sp_ready, ns + 1)
                    mm = pe.matmul(ps[:, zi % 4, 0:W], c(NEG_TRI), sp[:, ns % 3, 0:W], start=False, stop=True,
                                   skip_group_check=True)
                    if b < TT - 1:
                        pe.wait_ge(cum_done, 3 * (ns // 4) + (TT - 1 - b))
                        mm = pe.matmul(ps[:, zi % 4, P:W], c(NEG_ONES), cum[:, (b + 1) % 3, b * P:T - P],
                                       start=False, stop=True, skip_group_check=True)
                    mm.then_inc(s_done, 1)
                    ns += 1
                elif ev[0] == "o":
                    p, hh, b = ev[1]
                    W = T - b * P
                    if hh < 2:
                        pe.wait_ge(w_masked, sb_tiles.index(ev[1]) + 1)
                        if hh == 0 and b == TT - 1 and p:
                            pe.wait_ge(osb_lo_done, p)
                        o = ps[hh * SBD:(hh + 1) * SBD, O_SB, b * P:T]
                        vv = v_sb[:, b, p * P + hh * SBD:p * P + (hh + 1) * SBD]
                    else:
                        pe.wait_ge(w_ret, ret_tiles.index(ev[1]) + 1)
                        if b == TT - 1 and p:
                            pe.wait_ge(gn_std, p)
                        o = ps[:, O_RET, b * P:T]
                        vv = v_r[:, b, p * P:(p + 1) * P]
                    pe.matmul(o, vv, wt[:, no % 4, 0:W], start=(b == TT - 1), stop=True,
                              skip_group_check=True).then_inc(o_done, 1)
                    no += 1
                elif ev[0] == "gate":
                    j, k = ev[1], ev[2]
                    if k == 0:
                        pe.wait_ge(w_lo_done, U_MERGE + j + 1)
                        evacuated(len(FILLS) - 2 + j)
                    mm = product(GATE_BANK[j], (j, k * P), h_hi[:, k, :], h_lo[:, k, :], k == 0, k == KD - 1)
                    if k == KD - 1:
                        mm.then_inc(unit_done, 1)
                elif ev[0] == "gn_b":
                    pe.wait_ge(gn_copied, ev[1] + 1)
                    pe.matmul(ps[:, O_RET, :], c(MEAN), gn_t[:, :], start=True, stop=True).then_inc(gn_mean, 1)
                elif ev[0] == "gn_d":
                    pe.wait_ge(gn_squared, ev[1] + 1)
                    pe.matmul(ps[:, O_RET, :], c(MEAN), gn_t[:, :], start=True, stop=True).then_inc(gn_var, 1)

            pe.wait_ge(osb_lo_done, PAIRS)

            def merge(d, par, waits, first=0):
                for j, (hi, lo, nk) in enumerate(((h_hi, h_lo, KD), (h_hi, h_lo, KD),
                                                  (o_sb_hi, o_sb_lo, PAIRS), (o_r_hi, o_r_lo, RH))):
                    if j < first:
                        continue
                    if waits and j < 2:
                        pe.wait_ge(branch_scaled, d * 2 - 3 + j)
                    if waits and j >= 2:
                        pe.wait_ge(tm_done, d * 2 - 5 + j)
                    if not waits and par == 0 and j == 3:
                        pe.wait_ge(or_lo_done, RH)
                    unit(d * 4 + U_MERGE + j, j, merge_bank(par, j), hi, lo, nk)

            merge(0, 0, False, first=2)
            merge(1, 1, False)
            with pe.Fori(1, KD // 2) as turn:
                d = turn * 2
                for par in range(2):
                    merge(d + par, par, True)
            for d in range(KD):
                if d == 0:
                    pe.wait_ge(tm_done, 2 * KD)
                unit(U_OUT + d, d % SLOTS, d, m_hi, m_lo, each_k=(m_lo_done, 0) if d == 0 else None)
            post_stats(1)
            ffn(1, U_UP2)
            post_stats(2)
            for n in range(2 * TT):
                half, t = n // TT, n % TT
                for j in range(4):
                    k = 4 * half + j
                    if t == 0 and k % 2 == 0:
                        pe.wait_ge(x_ready, 2 * KD + k // 2 + 1)
                    elif t == 0:
                        pe.wait_ge(x_ready_v, k // 2 + 1)
                    mm = pe.transpose(ps[:, n, j * P:(j + 1) * P], xs[:, k, t * P:(t + 1) * P], c(IDENT))
                mm.then_inc(out_t, 1)

        @block.scalar
        def _(act_eng):
            act_eng.dma_start(cst[:, 0:CONST_COLS], const).then_inc(const_in, 16)
            for i, g in enumerate(gains):
                act_eng.dma_start(g_tok[i * KD:(i + 1) * KD, :], g.rearrange("(k p) -> k p", p=P)).then_inc(gains_in, 16)
            for t in (0, 2):
                act_eng.dma_start(x_tok[:, t, :], x[t * P:(t + 1) * P, :]).then_inc(x_in[t], 16)
            act_eng.dma_start(decay[:, :, :], decay_t).then_inc(tables_in, 16)
            act_eng.dma_start(rope[:, :, :], rope_t).then_inc(tables_in, 16)

            def split(u, slot, turn, cols=UNIT):
                act_eng.wait_ge(raw_full[slot], turn * 16 + 16)
                wait(act_eng, unit_done, u - (SLOTS - 1))
                act_eng.activation(w_hi[:, slot, 0:cols], w_raw[:, slot, 0:cols], ACT.Copy).then_inc(w_hi_done, 1)

            def split_u(u):
                if u < U_END:
                    split(u, u % SLOTS, u // SLOTS, unit_cols(u))

            def root(n, src):
                act_eng.activation(std[:, :], src, ACT.Sqrt, bias=cst[:, EPS:EPS + 1],
                                   scale=1.0 / D).then_inc(std_ready, 1)

            def post_norm(i, ready, raw_stream):
                for q, d in enumerate(Y_ORDER):
                    ready(q, d)
                    if q >= 3:
                        act_eng.wait_ge(yacc_done, 6 * i + max(q - 3, 1))
                    act_eng.activation(sq[:, q % 3, :], ps[:, d, :], ACT.Square).then_inc(ysq_ready, 1)
                if raw_stream:
                    act_eng.wait_ge(ms_ready, i + 1)
                    root(2 * i + 1, ms[:, :])
                else:
                    act_eng.wait_ge(stat_done, 2 * i + 2)
                    root(2 * i + 1, ps[:, R_POST, 0:TT])
                keep_r(2 * i + 1)

            def stream_in(i, ready):
                for k in range(KD + 1):
                    if k < KD:
                        ready(k)
                        act_eng.activation(h_hi[:, k, :], xs[:, k, :], ACT.Copy, scale=gcol[:, 2 * i, k:k + 1]
                                           ).then_inc(h_hi_done, 1)
                    if k >= 1:
                        act_eng.activation(ys[:, k - 1, :], xs[:, k - 1, :], ACT.Square).then_inc(xsq_ready, 1)

            def pre_root(i):
                act_eng.wait_ge(stat_done, 2 * i + 1)
                root(2 * i, ps[:, R_PRE, 0:TT])

            def keep_r(n):
                act_eng.wait_ge(r_ready, n + 1)
                act_eng.activation(r_all[:, :], ps[:, R_POST if n % 2 else R_PRE, :], ACT.Copy
                                   ).then_inc(r_all_ready, 1)

            def ffn_out(fi, ud):
                def ready(q, d):
                    if q < KD - 1:
                        act_eng.wait_ge(y_ready, (KD - 1) * fi + q + 1)
                    else:
                        act_eng.wait_ge(unit_done, ud + NF)
                return ready

            def ffn(fi, u0):
                def silu(f, j):
                    act_eng.wait_ge(gate_scaled, f + NF * fi + 1)
                    act_eng.activation(gate_s[:, j, :], gate_s[:, j, :], ACT.Silu).then_inc(silu_done, 1)

                def step(f, j, turn):
                    for q in range(2):
                        v = 2 * j + q + AHEAD
                        split(f * 2 + u0 + q + AHEAD, v % SLOTS, turn + v // SLOTS)
                        if q == 0:
                            silu(f, j)

                def part(f, par):
                    act_eng.wait_ge(a_done, f + NF * fi + 1)
                    wait(act_eng, unit_done, f + u0 + 2 * NF - 1)
                    act_eng.activation(a_hi[:, par, :], act[:, f, :], ACT.Copy).then_inc(a_hi_done, 1)

                split_u(u0 + AHEAD)
                split_u(u0 + AHEAD + 1)
                pre_root(2 * fi)
                split_u(u0 + AHEAD + 2)
                split_u(u0 + AHEAD + 3)
                keep_r(4 * fi)
                silu(0, 0)
                silu(1, 1)
                part0(fi)
                with act_eng.Fori(1, NF // 2) as i:
                    for j in range(2):
                        step(i * 2 + j, j, i + u0 // SLOTS)
                ud = u0 + 2 * NF
                split_u(ud + AHEAD)
                part(1, 1)
                with act_eng.Fori(0, (NF - 4) // SLOTS) as i:
                    for j in range(1, SLOTS + 1):
                        v = j + AHEAD
                        split(i * 4 + ud + v, v % SLOTS, i + ud // SLOTS + v // SLOTS)
                        part(i * 4 + j + 1, (j + 1) % 2)
                for f in range(NF - 3, NF):
                    split_u(ud + f + AHEAD)
                    if f + 1 < NF:
                        part(f + 1, (f + 1) % 2)

            def part0(fi):
                act_eng.wait_ge(a_done, NF * fi + 1)
                act_eng.activation(a_hi[:, 0, :], act[:, 0, :], ACT.Copy).then_inc(a_hi_done, 1)

            for k in range(1, KD, 2):
                act_eng.wait_ge(xt_done, k + 1)
                act_eng.activation(xs[:, k, :], ps[:, k, :], ACT.Copy).then_inc(x_copied[1], 1)
                if k in (1, 3):
                    split_u(k // 2)
            act_eng.wait_ge(gains_ok, 1)
            stream_in(0, lambda k: act_eng.wait_ge(x_copied[k % 2], k // 2 + 1))
            ffn(0, U_UP1)
            post_norm(0, ffn_out(0, U_DOWN1), True)
            stream_in(1, lambda k: act_eng.wait_ge(x_ready, k + 1))
            split_u(U_V + AHEAD)
            split_u(U_V + AHEAD + 1)
            split_u(U_V + AHEAD + 2)
            pre_root(1)
            split_u(U_V + AHEAD + 3)
            keep_r(2)
            act_eng.wait_ge(rstd_ready, 2 + 1)

            for kind in range(2):
                for j in range(4 if kind else 0):
                    split_u(U_V + 4 * kind + j + AHEAD)
                for t in (1, 3):
                    dst = v_sb if kind == 0 else v_r
                    if t < 3:
                        act_eng.wait_ge(v_ready, 3 * kind + t + 1)
                    else:
                        act_eng.wait_ge(unit_done, U_V + 4 * kind + 4)
                    act_eng.activation(dst[:, t, :], ps[:, 4 * kind + t, :], ACT.Copy, scale=r_tok[:, t:t + 1]
                                       ).then_inc(v_copied, 1)

            act_eng.preload_act_table_set("natural_log_exp_and_others")
            nz = nl = nw = chain = 0
            for ev in events:
                if ev[0] == "mm" and ev[2] == 0:
                    split_u(U_HEADS + ev[1] + AHEAD)
                if ev[0] == "gate" and ev[2] == 0:
                    split_u(U_MERGE + ev[1] + AHEAD)
                if ev[0] == "mm" and ev[2] == KD - 1:
                    f = ev[1]
                    kind, s = FILLS[f]
                    if kind in ("q", "k"):
                        j = "qk".index(kind)
                        act_eng.wait_ge(q_scaled, 2 * s + j + 1)
                        if s >= 2:
                            act_eng.wait_ge(z_ready, 12 * (s - 2) + 8)
                        act_eng.activation(qk_hi[:, s % 2, j, :], proj_t[:, :], ACT.Copy).then_inc(q_hi_done, 1)
                elif ev[0] == "z":
                    p, hh, b = ev[1]
                    W = T - b * P
                    if hh < 2:
                        act_eng.wait_ge(z_ready, nz + 1)
                        wait(act_eng, s_done, nl - 2)
                        wait(act_eng, cum_done, cum_count(nl - 3))
                        l = sp[:, nl % 3, 0:W]
                        act_eng.activation(l, ps[:, nz % 4, 0:W], ACT.Abs).then_inc(l_step, 1)
                        act_eng.wait_ge(l_step, 3 * nl + 1)
                        act_eng.activation(l, l, ACT.Exp, scale=-1.0).then_inc(l_step, 1)
                        act_eng.wait_ge(l_step, 3 * nl + 2)
                        act_eng.activation(l, l, ACT.Ln, bias=1.0).then_inc(l_step, 1)
                        nl += 1
                    nz += 1
                elif ev[0] == "s":
                    p, hh, b = ev[1]
                    W = T - b * P
                    zi = score_tiles.index(ev[1])
                    act_eng.wait_ge(s_done, nw + 1)
                    wait(act_eng, o_done, zi - 3)
                    act_eng.activation(wt[:, zi % 4, 0:W], ps[:, zi % 4, 0:W], ACT.Exp).then_inc(w_raw_done, 1)
                    nw += 1
                elif ev[0] == "sb_out":
                    p = ev[1]
                    act_eng.wait_ge(o_done, 12 * p + 8)
                    act_eng.activation(o_sb_hi[:, p, :], ps[:, O_SB, :], ACT.Copy).then_inc(osb_hi_done, 1)
                elif ev[0] == "gn_a":
                    p = ev[1]
                    act_eng.wait_ge(o_done, 12 * (p + 1))
                    wait(act_eng, or_lo_done, p)
                    act_eng.activation(gn_t[:, :], ps[:, O_RET, :], ACT.Copy).then_inc(gn_copied, 1)
                elif ev[0] == "gn_c":
                    act_eng.wait_ge(gn_centred, ev[1] + 1)
                    act_eng.activation(gn_t[:, :], gn_c[:, :], ACT.Square).then_inc(gn_squared, 1)
                elif ev[0] == "gn_e":
                    p = ev[1]
                    act_eng.wait_ge(gn_var, p + 1)
                    act_eng.activation(gn_t[:, :], ps[:, O_RET, :], ACT.Sqrt, bias=cst[:, EPS + 1:EPS + 2]
                                       ).then_inc(gn_std, 1)
                    act_eng.wait_ge(g_copied, p + 1)
                    act_eng.activation(g_r[:, :], g_r[:, :], ACT.Silu).then_inc(gn_silu, 1)
                    act_eng.preload_act_table_set("natural_log_exp_and_others")
                elif ev[0] == "gn_f":
                    p = ev[1]
                    act_eng.wait_ge(gn_v, 3 * p + 3)
                    act_eng.activation(o_r_hi[:, p, :], gn_t[:, :], ACT.Copy).then_inc(or_hi_done, 1)

            def merge(d, par, waits, first=0):
                for j in range(4):
                    v = j + AHEAD
                    if j >= first:
                        split(d * 4 + U_MERGE + v, v % SLOTS, d + U_MERGE // SLOTS + v // SLOTS, half_units(v))
                    if j < 2:
                        act_eng.wait_ge(branch_scaled, d * 2 + j + 1)
                        act_eng.activation(sig[:, 2 * par + j, :], sig[:, 2 * par + j, :], ACT.Sigmoid
                                           ).then_inc(sig_done, 1)
                act_eng.wait_ge(m_done, d + 1)
                act_eng.activation(m_hi[:, d, :], tm[:, par, 0, :], ACT.Copy).then_inc(m_hi_done, 1)

            merge(0, 0, False, first=2)
            merge(1, 1, False)
            with act_eng.Fori(1, KD // 2) as turn:
                d = turn * 2
                for par in range(2):
                    merge(d + par, par, True)
            for d in range(KD):
                split_u(U_OUT + d + AHEAD)
            post_norm(1, lambda q, d: act_eng.wait_ge(unit_done, U_OUT + d + 1), False)
            stream_in(2, lambda k: act_eng.wait_ge(x_ready, KD + k + 1))
            ffn(1, U_UP2)
            post_norm(2, ffn_out(1, U_DOWN2), True)
            for n in range(1, 2 * TT, 2):
                half, t = n // TT, n % TT
                act_eng.wait_ge(out_t, n + 1)
                act_eng.activation(x_tok[:, t, half * T:(half + 1) * T], ps[:, n, :], ACT.Copy
                                   ).then_inc(out_copied[1], 1)

        @block.vector
        def _(dve):
            def split(u, slot, cols=UNIT):
                dve.wait_ge(w_hi_done, u + 1)
                dve.tensor_tensor(w_lo[:, slot, 0:cols], w_raw[:, slot, 0:cols],
                                  w_hi[:, slot, 0:cols].bitcast(F32), ALU.subtract).then_inc(w_lo_done, 1)

            def split_u(u):
                if u < U_END:
                    split(u, u % SLOTS, unit_cols(u))

            def diagonal(n, src, factor):
                for j in range(TT):
                    op = dve.tensor_scalar(diag[:, j, :], c(IDENT), src[:, j:j + 1], factor, ALU.mult, ALU.mult)
                op.then_inc(diag_ready, 1)

            def pre_rstd(i):
                dve.wait_ge(std_ready, 2 * i + 1)
                dve.reciprocal(r_tok[:, :], std[:, :]).then_inc(rstd_ready, 1)
                dve.wait_ge(rstd_ready, 2 * i + 1)
                diagonal(2 * i, r_tok, 1.0)
                dve.tensor_tensor(r_tok2[:, :], r_tok[:, :], r_tok[:, :], ALU.mult)

            def scale_y(i, k):
                src = ys if k == R_POST else ps
                dve.scalar_tensor_tensor(out=ys[:, k, :], in0=src[:, k, :], scalar=gcol[:, 2 * i + 1, k:k + 1],
                                         in1=r_all[:, :], op0=ALU.mult, op1=ALU.mult).then_inc(y_scaled, 1)

            def stream_lo(i, k):
                dve.wait_ge(h_hi_done, KD * i + k + 1)
                dve.scalar_tensor_tensor(out=h_lo[:, k, :], in0=xs[:, k, :], scalar=gcol[:, 2 * i, k:k + 1],
                                         in1=h_hi[:, k, :].bitcast(F32), op0=ALU.mult, op1=ALU.subtract
                                         ).then_inc(h_lo_done, 1)

            def sum_squares(i):
                for m, k in enumerate((3, 5, 7)):
                    dve.wait_ge(xsq_ready, KD * i + k + 1)
                    wait(dve, xacc_v, 4 * i + m)
                    dve.tensor_tensor(ys[:, 1, :], ys[:, 1, :], ys[:, k, :], ALU.add).then_inc(xacc_v, 1)
                dve.wait_ge(xacc_p, 3 * (i + 1))
                dve.wait_ge(xacc_v, 4 * i + 3)
                dve.tensor_tensor(ys[:, 1, :], ys[:, 1, :], ys[:, 0, :], ALU.add).then_inc(xacc_v, 1)

            def post_norm(i, raw_stream):
                n = 2 * i + 1
                dve.wait_ge(ysq_ready, KD * i + 1)
                dve.tensor_copy(ys[:, R_POST, :], ps[:, R_POST, :]).then_inc(y_kept, 1)
                for q in range(1, KD - 1):
                    dve.wait_ge(ysq_ready, KD * i + q + 1)
                    if q > 1:
                        dve.wait_ge(yacc_done, 6 * i + q - 1)
                    dve.tensor_tensor(acc[:, :], sq[:, 0, :] if q == 1 else acc[:, :], sq[:, q % 3, :], ALU.add
                                      ).then_inc(yacc_done, 1)
                if raw_stream:
                    dve.wait_ge(stat_done, n + 1)
                    dve.tensor_tensor(ms[:, :], ps[:, R_POST, 0:TT], r_tok2[:, :], ALU.mult).then_inc(ms_ready, 1)
                dve.wait_ge(std_ready, n + 1)
                dve.reciprocal(rstd[:, :], std[:, :]).then_inc(rstd_ready, 1)
                dve.wait_ge(rstd_ready, n + 1)
                if raw_stream:
                    dve.tensor_tensor(std[:, :], rstd[:, :], r_tok[:, :], ALU.mult).then_inc(ms_ready, 1)
                    dve.wait_ge(ms_ready, i + 2)
                diagonal(n, std if raw_stream else rstd, 0.5 if raw_stream else 1.0)
                dve.wait_ge(r_all_ready, n + 1)
                dve.wait_ge(y_kept, i + 1)

            def into_stream(i):
                for k in range(KD + 3):
                    if k < KD:
                        scale_y(i, k)
                    if k >= 3:
                        stream_lo(i + 1, k - 3)

            def ffn(fi, u0):
                def scale_gate(f, j):
                    dve.wait_ge(unit_done, f * 2 + u0 + 1)
                    wait(dve, a_done, NF * fi + f - 1)
                    dve.tensor_tensor(gate_s[:, j, :], ps[:, 2 * j, :], r_all[:, :], ALU.mult
                                      ).then_inc(gate_scaled, 1)

                def step(f, j, splits=True):
                    if splits:
                        split(f * 2 + u0 + AHEAD, (2 * j + AHEAD) % SLOTS)
                        scale_gate(f, j)
                        split(f * 2 + u0 + 1 + AHEAD, (2 * j + 1 + AHEAD) % SLOTS)
                    dve.wait_ge(silu_done, f + NF * fi + 1)
                    dve.wait_ge(unit_done, f * 2 + u0 + 2)
                    dve.tensor_tensor(act[:, f, :], gate_s[:, j, :], ps[:, 2 * j + 1, :], ALU.mult
                                      ).then_inc(a_done, 1)

                def part(f, par):
                    dve.wait_ge(a_hi_done, f + NF * fi + 1)
                    dve.tensor_tensor(a_lo[:, par, :], act[:, f, :], a_hi[:, par, :].bitcast(F32),
                                      ALU.subtract).then_inc(a_lo_done, 1)

                split_u(u0 + AHEAD)
                split_u(u0 + AHEAD + 1)
                sum_squares(2 * fi)
                pre_rstd(2 * fi)
                split_u(u0 + AHEAD + 2)
                split_u(u0 + AHEAD + 3)
                dve.wait_ge(r_all_ready, 4 * fi + 1)
                for j in range(2):
                    scale_gate(j, j)
                for j in range(2):
                    step(j, j, False)
                part(0, 0)
                with dve.Fori(1, NF // 2) as turn:
                    i = turn * 2
                    for j in range(2):
                        step(i + j, j)
                ud = u0 + 2 * NF
                split_u(ud + AHEAD)
                part(1, 1)
                with dve.Fori(0, (NF - 4) // SLOTS) as turn:
                    i = turn * SLOTS
                    for j in range(1, SLOTS + 1):
                        split(i + ud + j + AHEAD, (j + AHEAD) % SLOTS)
                        part(i + j + 1, (j + 1) % 2)
                for f in range(NF - 3, NF):
                    split_u(ud + f + AHEAD)
                    if f + 1 < NF:
                        part(f + 1, (f + 1) % 2)

            dve.wait_ge(gains_t, 1)
            dve.tensor_copy(gcol[:, :, :].rearrange("p g k -> p (g k)"), ps[:, 0, 0:6 * KD]).then_inc(gains_ok, 1)
            for k in range(0, KD, 2):
                dve.wait_ge(xt_done, k + 1)
                dve.tensor_copy(xs[:, k, :], ps[:, k, :]).then_inc(x_copied[0], 1)
                if k in (2, 4):
                    split_u(k // 2 - 1)
            dve.wait_ge(gains_ok, 1)
            for k in range(KD):
                if k % 2:
                    dve.wait_ge(x_copied[1], k // 2 + 1)
                stream_lo(0, k)
            ffn(0, U_UP1)
            post_norm(0, True)
            into_stream(0)
            split_u(U_V + AHEAD)
            split_u(U_V + AHEAD + 1)
            sum_squares(1)
            split_u(U_V + AHEAD + 2)
            pre_rstd(1)
            split_u(U_V + AHEAD + 3)

            for kind in range(2):
                for j in range(4 if kind else 0):
                    split_u(U_V + 4 * kind + j + AHEAD)
                for t in (0, 2):
                    dst = v_sb if kind == 0 else v_r
                    dve.wait_ge(v_ready, 3 * kind + t + 1)
                    dve.tensor_scalar(dst[:, t, :], ps[:, 4 * kind + t, :], r_tok[:, t:t + 1], None, ALU.mult
                                      ).then_inc(v_copied, 1)

            dve.wait_ge(tables_in, 32)
            dve.wait_ge(r_all_ready, 3)
            for j in range(2):
                dve.tensor_tensor(rope[:, j, :], rope[:, j, :], r_all[:, :], ALU.mult).then_inc(rope_scaled, 1)
            dve.wait_ge(rope_scaled, 2)
            nz = nl = nret = nrope = 0
            for ev in events:
                if ev[0] == "mm" and ev[2] == 0:
                    split_u(U_HEADS + ev[1] + AHEAD)
                if ev[0] == "gate" and ev[2] == 0:
                    split_u(U_MERGE + ev[1] + AHEAD)
                if ev[0] == "mm" and ev[2] == KD - 1:
                    f = ev[1]
                    kind, s = FILLS[f]
                    bank = ps[:, FILL + f % 2, :]
                    if kind in ("q", "k"):
                        j = "qk".index(kind)
                        dve.wait_ge(unit_done, U_HEADS + f + 1)
                        wait(dve, rope_done, nrope)
                        wait(dve, q_lo_done, 2 * s + j)
                        dve.scalar_tensor_tensor(out=proj_t[:, :], in0=bank, scalar=SBD ** -0.5 if j == 0 else 1.0,
                                                 in1=r_all[:, :], op0=ALU.mult, op1=ALU.mult).then_inc(q_scaled, 1)
                        dve.wait_ge(q_hi_done, 2 * s + j + 1)
                        dve.tensor_tensor(qk_lo[:, s % 2, j, :], proj_t[:, :], qk_hi[:, s % 2, j, :].bitcast(F32),
                                          ALU.subtract).then_inc(q_lo_done, 1)
                    elif kind == "g":
                        dve.wait_ge(unit_done, U_HEADS + f + 1)
                        wait(dve, gn_v, 3 * s)
                        dve.tensor_tensor(g_r[:, :], bank, r_all[:, :], ALU.mult).then_inc(g_copied, 1)
                    elif kind in ("qr", "kr"):
                        j = ("qr", "kr").index(kind)
                        dve.wait_ge(unit_done, U_HEADS + f + 1)
                        wait(dve, rope_done, nrope)
                        wait(dve, q_lo_done, 2 * s + 2)
                        wait(dve, z_ready, 12 * s)
                        lo, hi = slice(0, RD // 2), slice(RD // 2, RD)
                        dve.tensor_tensor(qk_r[:, j, :], bank, rope[:, 0, :], ALU.mult).then_inc(rope_mul, 1)
                        dve.tensor_tensor(proj_t[lo, :], ps[hi, FILL + f % 2, :], rope[hi, 1, :], ALU.mult
                                          ).then_inc(rope_mul, 1)
                        dve.tensor_tensor(proj_t[hi, :], ps[lo, FILL + f % 2, :], rope[lo, 1, :], ALU.mult
                                          ).then_inc(rope_mul, 1)
                        nrope += 1
                elif ev[0] == "z":
                    p, hh, b = ev[1]
                    W = T - b * P
                    if hh < 2:
                        dve.wait_ge(l_step, 3 * nl + 3)
                        dve.scalar_tensor_tensor(out=sp[:, nl % 3, 0:W], in0=ps[:, nz % 4, 0:W], scalar=0.0,
                                                 in1=sp[:, nl % 3, 0:W], op0=ALU.max, op1=ALU.add
                                                 ).then_inc(sp_raw, 1)
                        nl += 1
                    else:
                        dve.wait_ge(z_ready, nz + 1)
                        wait(dve, o_done, nz - 3)
                        dve.tensor_tensor(wt[:, nz % 4, 0:W], ps[:, nz % 4, 0:W], decay[:, p, 0:W], ALU.mult
                                          ).then_inc(w_ret, 1)
                        nret += 1
                    nz += 1
                elif ev[0] == "sb_out":
                    p = ev[1]
                    dve.wait_ge(osb_hi_done, p + 1)
                    dve.tensor_tensor(o_sb_lo[:, p, :], ps[:, O_SB, :], o_sb_hi[:, p, :].bitcast(F32), ALU.subtract
                                      ).then_inc(osb_lo_done, 1)
                elif ev[0] == "gn_c":
                    p = ev[1]
                    dve.wait_ge(gn_mean, p + 1)
                    dve.tensor_tensor(gn_c[:, :], gn_t[:, :], ps[:, O_RET, :], ALU.subtract).then_inc(gn_centred, 1)
                elif ev[0] == "gn_e":
                    p = ev[1]
                    dve.wait_ge(gn_std, p + 1)
                    dve.reciprocal(gn_t[:, :], gn_t[:, :]).then_inc(gn_v, 1)
                    dve.wait_ge(gn_v, 3 * p + 1)
                    dve.tensor_tensor(gn_c[:, :], gn_c[:, :], gn_t[:, :], ALU.mult).then_inc(gn_v, 1)
                    dve.wait_ge(gn_v, 3 * p + 2)
                    dve.wait_ge(gn_silu, p + 1)
                    dve.tensor_tensor(gn_t[:, :], gn_c[:, :], g_r[:, :], ALU.mult).then_inc(gn_v, 1)
                elif ev[0] == "gn_f":
                    p = ev[1]
                    dve.wait_ge(or_hi_done, p + 1)
                    dve.tensor_tensor(o_r_lo[:, p, :], gn_t[:, :], o_r_hi[:, p, :].bitcast(F32), ALU.subtract
                                      ).then_inc(or_lo_done, 1)

            def merge(d, par, waits, first=0):
                for j in range(4):
                    v = j + AHEAD
                    if j >= first:
                        split(d * 4 + U_MERGE + v, v % SLOTS, half_units(v))
                    if j < 2:
                        dve.wait_ge(unit_done, d * 4 + U_MERGE + j + 1)
                        if waits:
                            dve.wait_ge(tm_done, d * 2 - 3 + j)
                        dve.tensor_tensor(sig[:, 2 * par + j, :], ps[:, merge_bank(par, j), :], r_all[:, :], ALU.mult
                                          ).then_inc(branch_scaled, 1)
                    if j >= 2:
                        dve.wait_ge(unit_done, d * 4 + U_MERGE + j + 1)
                        dve.wait_ge(sig_done, d * 2 + j - 1)
                        if waits and j == 2:
                            dve.wait_ge(m_lo_done, d - 1)
                        dve.tensor_tensor(tm[:, par, j - 2, :], sig[:, 2 * par + j - 2, :], ps[:, merge_bank(par, j), :],
                                          ALU.mult).then_inc(tm_done, 1)
                dve.wait_ge(tm_done, d * 2 + 2)
                dve.tensor_tensor(tm[:, par, 0, :], tm[:, par, 0, :], tm[:, par, 1, :], ALU.add).then_inc(m_done, 1)
                dve.wait_ge(m_hi_done, d + 1)
                dve.tensor_tensor(m_lo[:, d, :], tm[:, par, 0, :], m_hi[:, d, :].bitcast(F32), ALU.subtract
                                  ).then_inc(m_lo_done, 1)

            merge(0, 0, False, first=2)
            merge(1, 1, False)
            with dve.Fori(1, KD // 2) as turn:
                d = turn * 2
                for par in range(2):
                    merge(d + par, par, True)

            for d in range(KD):
                split_u(U_OUT + d + AHEAD)
            post_norm(1, False)
            into_stream(1)
            ffn(1, U_UP2)
            post_norm(2, True)
            for k in range(KD):
                scale_y(2, k)
                if k % 2 == 1:
                    dve.wait_ge(y_scaled, 2 * KD + k + 1)
                    dve.tensor_tensor(xs[:, k, :], xs[:, k, :], ys[:, k, :], ALU.add).then_inc(x_ready_v, 1)
            for n in range(0, 2 * TT, 2):
                half, t = n // TT, n % TT
                dve.wait_ge(out_t, n + 1)
                dve.tensor_copy(x_tok[:, t, half * T:(half + 1) * T], ps[:, n, :]).then_inc(out_copied[0], 1)

        @block.gpsimd
        def _(pool):
            def residual(i, step=1):
                for k in range(0, KD, step):
                    pool.wait_ge(y_scaled, KD * i + k + 1)
                    pool.tensor_tensor(xs[:, k, :], xs[:, k, :], ys[:, k, :], ALU.add).then_inc(x_ready, 1)

            def sum_squares(i):
                for m, k in enumerate((2, 4, 6)):
                    pool.wait_ge(xsq_ready, KD * i + k + 1)
                    wait(pool, xacc_p, 3 * i + m)
                    pool.tensor_tensor(ys[:, 0, :], ys[:, 0, :], ys[:, k, :], ALU.add).then_inc(xacc_p, 1)

            sum_squares(0)
            residual(0)
            sum_squares(1)
            nl = nw = nrope = 0
            for ev in events:
                if ev[0] == "mm" and ev[2] == KD - 1 and FILLS[ev[1]][0] in ("qr", "kr"):
                    j = ("qr", "kr").index(FILLS[ev[1]][0])
                    pool.wait_ge(rope_mul, 3 * nrope + 3)
                    pool.tensor_tensor(qk_r[:, j, :], qk_r[:, j, :], proj_t[:, :], ALU.add
                                       ).then_inc(rope_done, 1)
                    nrope += 1
                elif ev[0] == "z" and ev[1][1] < 2:
                    b = ev[1][2]
                    pool.wait_ge(sp_raw, nl + 1)
                    pool.affine_select(out=sp[:, nl % 3, 0:P], in_=sp[:, nl % 3, 0:P], pattern=[[1, P]],
                                       compare_op=ALU.is_gt, fill=0.0, base=0, channel_multiplier=-1
                                       ).then_inc(sp_ready, 1)
                    if b > 0:
                        pool.wait_ge(sp_ready, nl + 1)
                        wait(pool, s_done, nl - 1)
                        wait(pool, cum_done, 3 * (nl // 4) + TT - 1 - b)
                        new = cum[:, b % 3, :]
                        if b == TT - 1:
                            pool.tensor_copy(new[:, (b - 1) * P:b * P], sp[:, nl % 3, 0:P]).then_inc(cum_done, 1)
                        else:
                            pool.tensor_copy(new[:, (b - 1) * P:b * P], sp[:, nl % 3, 0:P])
                            pool.tensor_tensor(new[:, b * P:T - P], cum[:, (b + 1) % 3, b * P:T - P],
                                               sp[:, nl % 3, P:T - b * P], ALU.add).then_inc(cum_done, 1)
                    nl += 1
                elif ev[0] == "s":
                    zi = score_tiles.index(ev[1])
                    pool.wait_ge(w_raw_done, nw + 1)
                    pool.affine_select(out=wt[:, zi % 4, 0:P], in_=wt[:, zi % 4, 0:P], pattern=[[1, P]],
                                       compare_op=ALU.is_gt, fill=0.0, base=0, channel_multiplier=-1
                                       ).then_inc(w_masked, 1)
                    nw += 1
            residual(1)
            sum_squares(2)
            residual(2, 2)


_WEIGHTS = ("w_ffn1_gate", "w_ffn1_up", "w_ffn1_down", "w_in", "w_proj_sb", "w_proj_ret", "w_out",
            "w_ffn2_gate", "w_ffn2_up", "w_ffn2_down")
_GAINS = ("g_ffn1_pre", "g_ffn1_post", "g_mix_pre", "g_mix_post", "g_ffn2_pre", "g_ffn2_post")


def kernel(**inputs):
    import concourse.bacc as bacc
    from concourse.bass_utils import run_bass_kernel_spmd

    nc = bacc.Bacc("TRN2", target_bir_lowering=False, num_devices=1)
    arrays, aps = {}, {}

    def give(name, a):
        a = np.ascontiguousarray(a)
        arrays[name] = a
        aps[name] = nc.dram_tensor(name, a.shape, F32, kind="ExternalInput").ap()

    for name in ("x", *_WEIGHTS, *_GAINS):
        give(name, np.asarray(inputs[name])[0])
    for name, table in zip(("const", "decay_t", "rope_t"), constants()):
        give(name, table)
    out = nc.dram_tensor("out", (T, D), F32, kind="ExternalOutput").ap()
    build(nc, aps["x"], [aps[g] for g in _GAINS], *[aps[w] for w in _WEIGHTS],
          aps["const"], aps["decay_t"], aps["rope_t"], out)
    r = run_bass_kernel_spmd(nc, [arrays], core_ids=[0])
    return r.results[0]["out"].reshape(1, T, D)
```
